# Optimizing a Trainium2 kernel written in Bass

```python
import math
import jax, jax.numpy as jnp
from jax import lax
import numpy as np

D_MODEL = 1024
BATCH = 1
SEQ = 256
DEPTH = 2

GRID_W = 64
CTX_LEN = 256
HEAD_DIM = 64
EPS = 1e-6
NEG = -1e30
FOURIER_WIDTH = D_MODEL // 2
FOURIER_GROUPS = 4
FOURIER_GROUP_CH = FOURIER_WIDTH // FOURIER_GROUPS
WIN_Q_HEADS = (D_MODEL // 2) // HEAD_DIM
WIN_KV_HEADS = 2
WIN_RADIUS = 128
WIN_BLOCK = 128
EV_IN_WIDTH = FOURIER_WIDTH + (WIN_Q_HEADS + 2 * WIN_KV_HEADS) * HEAD_DIM
EV_OUT_WIDTH = FOURIER_WIDTH + WIN_Q_HEADS * HEAD_DIM
NA_HEADS = D_MODEL // HEAD_DIM
NA_KH = 8
NA_KW = 16
ROPE_THETA = 10000.0
ROPE_FREQS = HEAD_DIM // 4
D_FF = ((8 * D_MODEL // 3 + 255) // 256) * 256
N_EVEN = (DEPTH + 1) // 2
N_ODD = DEPTH // 2


def _rms(x, g):
    x32 = x.astype(jnp.float32)
    y = x32 * lax.rsqrt(jnp.mean(x32 * x32, axis=-1, keepdims=True) + EPS)
    return (y * g.astype(jnp.float32)).astype(x.dtype)

def _axial_angles(L):
    t = jnp.arange(L, dtype=jnp.int32)
    row = (t // GRID_W).astype(jnp.float32)
    col = (t % GRID_W).astype(jnp.float32)
    inv = ROPE_THETA ** (-jnp.arange(ROPE_FREQS, dtype=jnp.float32) / ROPE_FREQS)
    return row[:, None] * inv[None, :], col[:, None] * inv[None, :]

def _rotate(xa, ang):
    cos = jnp.cos(ang)[:, None, :].astype(xa.dtype)
    sin = jnp.sin(ang)[:, None, :].astype(xa.dtype)
    x1, x2 = xa[..., :ROPE_FREQS], xa[..., ROPE_FREQS:]
    return jnp.concatenate([x1 * cos - x2 * sin, x2 * cos + x1 * sin], axis=-1)

def _rope_2d(x, ang_row, ang_col):
    h = HEAD_DIM // 2
    return jnp.concatenate([_rotate(x[..., :h], ang_row), _rotate(x[..., h:], ang_col)], axis=-1)

def _fourier_mix(f):
    B, L, _ = f.shape
    fg = f.astype(jnp.float32).reshape(B, L, FOURIER_GROUPS, FOURIER_GROUP_CH)
    mixed = jnp.fft.fft2(fg, axes=(1, 3), norm="ortho").real
    return mixed.reshape(B, L, FOURIER_WIDTH).astype(f.dtype)

def _ctx_attention(q, k, v, sink):
    B, C, H, d = q.shape
    KV = k.shape[2]
    G = H // KV
    qg = q.reshape(B, C, KV, G, d)
    s = jnp.einsum('bqkgd,bjkd->bkgqj', qg, k).astype(jnp.float32) * (1.0 / math.sqrt(d))
    if sink is not None:
        sk = jnp.broadcast_to(sink.astype(jnp.float32).reshape(1, KV, G, 1, 1), (B, KV, G, C, 1))
        p = jax.nn.softmax(jnp.concatenate([s, sk], axis=-1), axis=-1)[..., :C]
    else:
        p = jax.nn.softmax(s, axis=-1)
    o = jnp.einsum('bkgqj,bjkd->bqkgd', p.astype(v.dtype), v)
    return o.reshape(B, C, H * d)

def _window_attention(q, k, v, k_ctx, v_ctx, sink):
    B, L, H, d = q.shape
    KV = k.shape[2]
    G = H // KV
    C = k_ctx.shape[1]
    nb = L // WIN_BLOCK
    nw = 3 * WIN_BLOCK
    scale = 1.0 / math.sqrt(d)
    qb = q.reshape(B, nb, WIN_BLOCK, KV, G, d)
    pad = ((0, 0), (WIN_BLOCK, WIN_BLOCK), (0, 0), (0, 0))
    kp = jnp.pad(k, pad).reshape(B, nb + 2, WIN_BLOCK, KV, d)
    vp = jnp.pad(v, pad).reshape(B, nb + 2, WIN_BLOCK, KV, d)
    kw = jnp.concatenate([kp[:, :-2], kp[:, 1:-1], kp[:, 2:]], axis=2)
    vw = jnp.concatenate([vp[:, :-2], vp[:, 1:-1], vp[:, 2:]], axis=2)
    s_win = jnp.einsum('bnqkgd,bnjkd->bnkgqj', qb, kw).astype(jnp.float32) * scale
    s_ctx = jnp.einsum('bnqkgd,bjkd->bnkgqj', qb, k_ctx).astype(jnp.float32) * scale
    blk = jnp.arange(nb, dtype=jnp.int32)[:, None, None] * WIN_BLOCK
    qpos = blk + jnp.arange(WIN_BLOCK, dtype=jnp.int32)[None, :, None]
    kpos = blk - WIN_BLOCK + jnp.arange(nw, dtype=jnp.int32)[None, None, :]
    mask = (jnp.abs(kpos - qpos) <= WIN_RADIUS) & (kpos >= 0) & (kpos < L)
    s_win = jnp.where(mask[None, :, None, None], s_win, NEG)
    sk = jnp.broadcast_to(sink.astype(jnp.float32).reshape(1, 1, KV, G, 1, 1), (B, nb, KV, G, WIN_BLOCK, 1))
    p = jax.nn.softmax(jnp.concatenate([s_win, s_ctx, sk], axis=-1), axis=-1).astype(v.dtype)
    o = (jnp.einsum('bnkgqj,bnjkd->bnqkgd', p[..., :nw], vw)
         + jnp.einsum('bnkgqj,bjkd->bnqkgd', p[..., nw:nw + C], v_ctx))
    return o.reshape(B, L, H * d)

def _neighbourhood_attention(q, k, v, k_ctx, v_ctx, rel_bias):
    B, L, H, d = q.shape
    rows = L // GRID_W
    kh = min(NA_KH, rows)
    n = kh * GRID_W
    scale = 1.0 / math.sqrt(d)
    qg = q.reshape(B, rows, GRID_W, H, d)
    kg = k.reshape(B, rows, GRID_W, H, d)
    vg = v.reshape(B, rows, GRID_W, H, d)
    cq = jnp.arange(GRID_W, dtype=jnp.int32)
    c0 = jnp.clip(cq - NA_KW // 2, 0, GRID_W - NA_KW)
    col_ok = (cq[None, :] >= c0[:, None]) & (cq[None, :] < c0[:, None] + NA_KW)
    mask = jnp.tile(col_ok, (1, kh))
    dc_idx = jnp.clip(cq[None, :] - cq[:, None] + NA_KW - 1, 0, 2 * NA_KW - 2)

    def one_row(r):
        r0 = jnp.clip(r - kh // 2, 0, rows - kh)
        k_rows = lax.dynamic_slice_in_dim(kg, r0, kh, axis=1).reshape(B, n, H, d)
        v_rows = lax.dynamic_slice_in_dim(vg, r0, kh, axis=1).reshape(B, n, H, d)
        q_row = lax.dynamic_index_in_dim(qg, r, axis=1, keepdims=False)
        dr_idx = r0 + jnp.arange(kh, dtype=jnp.int32) - r + NA_KH - 1
        bias = rel_bias[:, dr_idx[None, :, None], dc_idx[:, None, :]]
        bias = bias.reshape(H, GRID_W, n).astype(jnp.float32)
        s_nb = jnp.einsum('bqhd,bjhd->bhqj', q_row, k_rows).astype(jnp.float32) * scale + bias[None]
        s_nb = jnp.where(mask[None, None], s_nb, NEG)
        s_cx = jnp.einsum('bqhd,bjhd->bhqj', q_row, k_ctx).astype(jnp.float32) * scale
        p = jax.nn.softmax(jnp.concatenate([s_nb, s_cx], axis=-1), axis=-1).astype(v.dtype)
        return (jnp.einsum('bhqj,bjhd->bqhd', p[..., :n], v_rows)
                + jnp.einsum('bhqj,bjhd->bqhd', p[..., n:], v_ctx))

    out = lax.map(one_row, jnp.arange(rows, dtype=jnp.int32))
    return out.transpose(1, 0, 2, 3, 4).reshape(B, L, H * d)

def _even_mixer(h, hc, w_in, w_out, q_g, k_g, sink, ang_row, ang_col, ctx_out):
    F = FOURIER_WIDTH
    QW = WIN_Q_HEADS * HEAD_DIM
    KW = WIN_KV_HEADS * HEAD_DIM

    def split(t):
        Bt, Lt = t.shape[0], t.shape[1]
        f = t[..., :F]
        q = _rms(t[..., F:F + QW].reshape(Bt, Lt, WIN_Q_HEADS, HEAD_DIM), q_g)
        k = _rms(t[..., F + QW:F + QW + KW].reshape(Bt, Lt, WIN_KV_HEADS, HEAD_DIM), k_g)
        v = t[..., F + QW + KW:].reshape(Bt, Lt, WIN_KV_HEADS, HEAD_DIM)
        return f, q, k, v

    f, q, k, v = split(h @ w_in)
    fc, qc, kc, vc = split(hc @ w_in)
    q = _rope_2d(q, ang_row, ang_col)
    k = _rope_2d(k, ang_row, ang_col)
    o = jnp.concatenate([_fourier_mix(f), _window_attention(q, k, v, kc, vc, sink)], axis=-1) @ w_out
    oc = None
    if ctx_out:
        oc = jnp.concatenate([_fourier_mix(fc), _ctx_attention(qc, kc, vc, sink)], axis=-1) @ w_out
    return o, oc

def _odd_mixer(h, hc, w_in, w_out, q_g, k_g, rel_bias, ctx_out):
    W = NA_HEADS * HEAD_DIM

    def split(t):
        Bt, Lt = t.shape[0], t.shape[1]
        q = _rms(t[..., :W].reshape(Bt, Lt, NA_HEADS, HEAD_DIM), q_g)
        k = _rms(t[..., W:2 * W].reshape(Bt, Lt, NA_HEADS, HEAD_DIM), k_g)
        v = t[..., 2 * W:].reshape(Bt, Lt, NA_HEADS, HEAD_DIM)
        return q, k, v

    q, k, v = split(h @ w_in)
    qc, kc, vc = split(hc @ w_in)
    o = _neighbourhood_attention(q, k, v, kc, vc, rel_bias) @ w_out
    oc = None
    if ctx_out:
        oc = _ctx_attention(qc, kc, vc, None) @ w_out
    return o, oc

def _swiglu(h, wg, wu, wd):
    return (jax.nn.silu(h @ wg) * (h @ wu)) @ wd

def first_inputs(seed: int = 0) -> dict:
    key = jax.random.key(seed)
    ks = jax.random.split(key, 24)
    D = D_MODEL
    nrm = jax.random.normal
    f32 = jnp.float32
    return {
        "x": nrm(ks[0], (BATCH, SEQ, D), f32),
        "c": nrm(ks[1], (BATCH, D), f32),
        "ctx": nrm(ks[2], (BATCH, CTX_LEN, D), f32),
        "c_ctx": nrm(ks[3], (D,), f32),
        "ada_w": nrm(ks[4], (DEPTH, D, 6 * D), f32) * D ** -0.5,
        "ada_b": nrm(ks[5], (DEPTH, 6 * D), f32) * 0.01,
        "norm1_g": 1.0 + 0.01 * nrm(ks[6], (DEPTH, D), f32),
        "norm2_g": 1.0 + 0.01 * nrm(ks[7], (DEPTH, D), f32),
        "ffn_w_gate": nrm(ks[8], (DEPTH, D, D_FF), f32) * D ** -0.5,
        "ffn_w_up": nrm(ks[9], (DEPTH, D, D_FF), f32) * D ** -0.5,
        "ffn_w_down": nrm(ks[10], (DEPTH, D_FF, D), f32) * D_FF ** -0.5,
        "ev_w_in": nrm(ks[11], (N_EVEN, D, EV_IN_WIDTH), f32) * D ** -0.5,
        "ev_w_out": nrm(ks[12], (N_EVEN, EV_OUT_WIDTH, D), f32) * EV_OUT_WIDTH ** -0.5,
        "ev_q_norm": 1.0 + 0.01 * nrm(ks[13], (N_EVEN, HEAD_DIM), f32),
        "ev_k_norm": 1.0 + 0.01 * nrm(ks[14], (N_EVEN, HEAD_DIM), f32),
        "ev_sink": 0.5 * nrm(ks[15], (N_EVEN, WIN_Q_HEADS), f32),
        "od_w_in": nrm(ks[16], (N_ODD, D, 3 * NA_HEADS * HEAD_DIM), f32) * D ** -0.5,
        "od_w_out": nrm(ks[17], (N_ODD, NA_HEADS * HEAD_DIM, D), f32) * (NA_HEADS * HEAD_DIM) ** -0.5,
        "od_q_norm": 1.0 + 0.01 * nrm(ks[18], (N_ODD, HEAD_DIM), f32),
        "od_k_norm": 1.0 + 0.01 * nrm(ks[19], (N_ODD, HEAD_DIM), f32),
        "od_rel_bias": 0.1 * nrm(ks[20], (N_ODD, NA_HEADS, 2 * NA_KH - 1, 2 * NA_KW - 1), f32),
    }

def first_block(x, c, ctx, c_ctx, ada_w, ada_b, norm1_g, norm2_g, ffn_w_gate, ffn_w_up, ffn_w_down,
              ev_w_in, ev_w_out, ev_q_norm, ev_k_norm, ev_sink,
              od_w_in, od_w_out, od_q_norm, od_k_norm, od_rel_bias):
    L = x.shape[1]
    ang_row, ang_col = _axial_angles(L)
    y = ctx
    for i in range(DEPTH):
        last = i == DEPTH - 1
        m_lat = (jax.nn.silu(c) @ ada_w[i] + ada_b[i])[:, None, :]
        m_ctx = jax.nn.silu(c_ctx) @ ada_w[i] + ada_b[i]
        sh1, sc1, g1, sh2, sc2, g2 = jnp.split(m_lat, 6, axis=-1)
        csh1, csc1, cg1, csh2, csc2, cg2 = jnp.split(m_ctx, 6, axis=-1)
        h = _rms(x, norm1_g[i]) * (1.0 + sc1) + sh1
        hc = _rms(y, norm1_g[i]) * (1.0 + csc1) + csh1
        if i % 2 == 0:
            j = i // 2
            o, oc = _even_mixer(h, hc, ev_w_in[j], ev_w_out[j], ev_q_norm[j], ev_k_norm[j],
                                ev_sink[j], ang_row, ang_col, not last)
        else:
            j = i // 2
            o, oc = _odd_mixer(h, hc, od_w_in[j], od_w_out[j], od_q_norm[j], od_k_norm[j],
                               od_rel_bias[j], not last)
        x = x + g1 * o
        h = _rms(x, norm2_g[i]) * (1.0 + sc2) + sh2
        x = x + g2 * _swiglu(h, ffn_w_gate[i], ffn_w_up[i], ffn_w_down[i])
        if not last:
            y = y + cg1 * oc
            hc = _rms(y, norm2_g[i]) * (1.0 + csc2) + csh2
            y = y + cg2 * _swiglu(hc, ffn_w_gate[i], ffn_w_up[i], ffn_w_down[i])
    return x


DEPTH_2 = 4

N_MIXERS = 3
N_RET_LAYERS = (DEPTH_2 + 2) // 3
N_CONV_LAYERS = (DEPTH_2 + 1) // 3
N_ATTN_LAYERS = DEPTH_2 // 3

RET_QK_DIM = 256
RET_HEADS = D_MODEL // RET_QK_DIM
RET_V_DIM = 2 * RET_QK_DIM
RET_CHUNK = 128
RET_ROPE_BASE = 10000.0
RET_QK_WIDTH = RET_HEADS * RET_QK_DIM
RET_V_WIDTH = RET_HEADS * RET_V_DIM
RET_IN_WIDTH = 2 * RET_QK_WIDTH + 2 * RET_V_WIDTH

CONV_WIDTH = 31
CONV_PAD = (CONV_WIDTH - 1) // 2

ATTN_HEAD_DIM = 64
ATTN_HEADS = D_MODEL // ATTN_HEAD_DIM
DILATION_GROUPS = ((128, 1), (512, 4), (2048, 16))
N_ATTN_GROUPS = len(DILATION_GROUPS)
ATTN_IN_WIDTH = N_ATTN_GROUPS * 3 * ATTN_HEADS * ATTN_HEAD_DIM
ROPE_THETA_2 = 500000.0
ROT_DIM = ATTN_HEAD_DIM // 4

FFN_HIDDEN = -(-8 * D_MODEL // (3 * 256)) * 256

RMS_EPS = 1e-6
LN_EPS = 1e-5
MASK_VALUE = -1e30


def _rmsnorm(x, g):
    xf = x.astype(jnp.float32)
    y = xf * lax.rsqrt(jnp.mean(xf * xf, axis=-1, keepdims=True) + RMS_EPS)
    return (y * g.astype(jnp.float32)).astype(x.dtype)

def _layernorm(x, g, b):
    xf = x.astype(jnp.float32)
    mu = jnp.mean(xf, axis=-1, keepdims=True)
    var = jnp.mean(jnp.square(xf - mu), axis=-1, keepdims=True)
    y = (xf - mu) * lax.rsqrt(var + LN_EPS)
    return (y * g.astype(jnp.float32) + b.astype(jnp.float32)).astype(x.dtype)

def _rotate_2(x, cos, sin):
    half = x.shape[-1] // 2
    x1, x2 = x[..., :half], x[..., half:]
    return jnp.concatenate([x1 * cos - x2 * sin, x2 * cos + x1 * sin], axis=-1).astype(x.dtype)

def _retention_dir(q, k, v, log1m_gamma, strict):
    B, H, S, dk = q.shape
    dv = v.shape[-1]
    C = RET_CHUNK
    n = S // C
    dt = v.dtype
    gamma = 1.0 - jnp.exp(log1m_gamma.astype(jnp.float32))
    lg = jnp.log(gamma)
    idx = jnp.arange(C)
    diff = idx[:, None] - idx[None, :]
    live = (diff > 0) if strict else (diff >= 0)
    dmat = jnp.where(live, jnp.exp(lg[:, None, None] * jnp.where(live, diff, 0)), 0.0)
    xi = jnp.exp(lg[:, None] * (idx + 1)[None, :]).astype(dt)
    zeta = jnp.exp(lg[:, None] * (C - 1 - idx)[None, :]).astype(dt)
    chunk_decay = jnp.exp(lg * C).astype(dt)

    qc = q.reshape(B, H, n, C, dk)
    kc = k.reshape(B, H, n, C, dk)
    vc = v.reshape(B, H, n, C, dv)
    scores = jnp.einsum('bhnid,bhnjd->bhnij', qc, kc) * dmat[None, :, None].astype(dt)
    intra = jnp.einsum('bhnij,bhnje->bhnie', scores, vc)

    def step(state, inp):
        qb, kb, vb = inp
        cross = jnp.einsum('bhcd,bhde->bhce', qb * xi[None, :, :, None], state)
        state = state * chunk_decay[None, :, None, None] + jnp.einsum(
            'bhcd,bhce->bhde', kb * zeta[None, :, :, None], vb)
        return state, cross

    state0 = jnp.zeros((B, H, dk, dv), dt)
    _, cross = lax.scan(step, state0, (jnp.moveaxis(qc, 2, 0), jnp.moveaxis(kc, 2, 0), jnp.moveaxis(vc, 2, 0)))
    out = intra + jnp.moveaxis(cross, 0, 2)
    return out.reshape(B, H, S, dv)

def _retention_mixer(h, w_in, log1m_decay, w_out):
    B, S, _ = h.shape
    proj = h @ w_in
    q = proj[..., :RET_QK_WIDTH]
    k = proj[..., RET_QK_WIDTH:2 * RET_QK_WIDTH]
    v = proj[..., 2 * RET_QK_WIDTH:2 * RET_QK_WIDTH + RET_V_WIDTH]
    g = proj[..., 2 * RET_QK_WIDTH + RET_V_WIDTH:]
    q = q.reshape(B, S, RET_HEADS, RET_QK_DIM).transpose(0, 2, 1, 3)
    k = k.reshape(B, S, RET_HEADS, RET_QK_DIM).transpose(0, 2, 1, 3)
    v = v.reshape(B, S, RET_HEADS, RET_V_DIM).transpose(0, 2, 1, 3)
    inv = 1.0 / (RET_ROPE_BASE ** jnp.linspace(0.0, 1.0, RET_QK_DIM // 2, dtype=jnp.float32))
    ang = jnp.arange(S, dtype=jnp.float32)[:, None] * inv[None, :]
    cos, sin = jnp.cos(ang), jnp.sin(ang)
    q = _rotate_2(q, cos, sin)
    k = (_rotate_2(k, cos, sin) * (RET_QK_DIM ** -0.5)).astype(h.dtype)
    fwd = _retention_dir(q, k, v, log1m_decay[0], strict=False)
    bwd = _retention_dir(q[:, :, ::-1], k[:, :, ::-1], v[:, :, ::-1], log1m_decay[1], strict=True)[:, :, ::-1]
    o = (fwd + bwd).astype(jnp.float32)
    o = o * lax.rsqrt(jnp.mean(o * o, axis=-1, keepdims=True) + RMS_EPS)
    o = o.transpose(0, 2, 1, 3).reshape(B, S, RET_V_WIDTH).astype(h.dtype)
    return (jax.nn.silu(g) * o) @ w_out

def _conv_mixer(h, w_in, b_in, w_dw, b_dw, ln_g, ln_b, w_out, b_out):
    a = h @ w_in + b_in
    u = a[..., :D_MODEL] * jax.nn.sigmoid(a[..., D_MODEL:])
    u = lax.conv_general_dilated(
        u, w_dw[:, None, :].astype(u.dtype), window_strides=(1,), padding=[(CONV_PAD, CONV_PAD)],
        dimension_numbers=('NWC', 'WIO', 'NWC'), feature_group_count=D_MODEL) + b_dw
    u = jax.nn.silu(_layernorm(u, ln_g, ln_b))
    return u @ w_out + b_out

def _dilated_band_attention(q, k, v, dil, radius):
    B, S, H, Dh = q.shape
    L = S // dil
    W = radius
    nb = -(-L // W)
    Lp = nb * W

    def strided(t):
        return t.reshape(B, L, dil, H, Dh).transpose(0, 2, 3, 1, 4)

    qs, ks, vs = strided(q), strided(k), strided(v)
    qs = jnp.pad(qs, ((0, 0), (0, 0), (0, 0), (0, Lp - L), (0, 0)))
    kvpad = ((0, 0), (0, 0), (0, 0), (W, Lp - L + W), (0, 0))
    kb = jnp.pad(ks, kvpad).reshape(B, dil, H, nb + 2, W, Dh)
    vb = jnp.pad(vs, kvpad).reshape(B, dil, H, nb + 2, W, Dh)
    qb = qs.reshape(B, dil, H, nb, W, Dh)
    kwin = jnp.concatenate([kb[:, :, :, 0:nb], kb[:, :, :, 1:nb + 1], kb[:, :, :, 2:nb + 2]], axis=4)
    vwin = jnp.concatenate([vb[:, :, :, 0:nb], vb[:, :, :, 1:nb + 1], vb[:, :, :, 2:nb + 2]], axis=4)
    blk = jnp.arange(nb)[:, None]
    qpos = blk * W + jnp.arange(W)[None, :]
    kpos = (blk - 1) * W + jnp.arange(3 * W)[None, :]
    mask = ((jnp.abs(qpos[:, :, None] - kpos[:, None, :]) <= radius)
            & (kpos[:, None, :] >= 0) & (kpos[:, None, :] < L))
    s = jnp.einsum('bghnqd,bghnkd->bghnqk', qb, kwin).astype(jnp.float32) * (Dh ** -0.5)
    s = jnp.where(mask, s, MASK_VALUE)
    mx = jnp.max(s, axis=-1, keepdims=True)
    p = jnp.exp(s - mx)
    den = jnp.sum(p, axis=-1)
    o = jnp.einsum('bghnqk,bghnkd->bghnqd', p.astype(v.dtype), vwin).astype(jnp.float32) / den[..., None]
    lse = mx[..., 0] + jnp.log(den)
    o = o.reshape(B, dil, H, Lp, Dh)[:, :, :, :L].transpose(0, 3, 1, 2, 4).reshape(B, S, H, Dh)
    lse = lse.reshape(B, dil, H, Lp)[:, :, :, :L].transpose(0, 3, 1, 2).reshape(B, S, H)
    return o, lse

def _dilated_attention_mixer(h, w_in, w_out):
    B, S, _ = h.shape
    proj = (h @ w_in).reshape(B, S, N_ATTN_GROUPS, 3, ATTN_HEADS, ATTN_HEAD_DIM)
    inv = ROPE_THETA_2 ** (-jnp.arange(0, ROT_DIM, 2, dtype=jnp.float32) / ROT_DIM)
    ang = jnp.arange(S, dtype=jnp.float32)[:, None] * inv[None, :]
    cos, sin = jnp.cos(ang)[:, None, :], jnp.sin(ang)[:, None, :]

    def prope(t):
        return jnp.concatenate([_rotate_2(t[..., :ROT_DIM], cos, sin), t[..., ROT_DIM:]], axis=-1)

    outs, lses = [], []
    for g, (window, dil) in enumerate(DILATION_GROUPS):
        q = prope(proj[:, :, g, 0])
        k = prope(proj[:, :, g, 1])
        v = proj[:, :, g, 2]
        o, l = _dilated_band_attention(q, k, v, dil, window // (2 * dil))
        outs.append(o)
        lses.append(l)
    wts = jax.nn.softmax(jnp.stack(lses, 0), axis=0)
    o = jnp.sum(wts[..., None] * jnp.stack(outs, 0), axis=0).astype(h.dtype)
    return o.reshape(B, S, ATTN_HEADS * ATTN_HEAD_DIM) @ w_out

def _swiglu_2(h, w_in, w_out):
    a = h @ w_in
    return (jax.nn.silu(a[..., :FFN_HIDDEN]) * a[..., FFN_HIDDEN:]) @ w_out

def second_inputs(seed: int = 0) -> dict:
    key = jax.random.key(seed)
    ks = jax.random.split(key, 20)
    f32 = jnp.float32
    nrm = lambda k, shape, scale: jax.random.normal(k, shape, f32) * scale
    base_decay = -(5.0 + jnp.arange(RET_HEADS, dtype=f32)) * np.float32(np.log(2.0))
    return {
        "x": nrm(ks[0], (BATCH, SEQ, D_MODEL), 1.0),
        "norm_w": 1.0 + nrm(ks[1], (DEPTH_2, 4, D_MODEL), 0.05),
        "ffn_w_in": nrm(ks[2], (DEPTH_2, D_MODEL, 2 * FFN_HIDDEN), D_MODEL ** -0.5),
        "ffn_w_out": nrm(ks[3], (DEPTH_2, FFN_HIDDEN, D_MODEL), FFN_HIDDEN ** -0.5),
        "ret_w_in": nrm(ks[4], (N_RET_LAYERS, D_MODEL, RET_IN_WIDTH), D_MODEL ** -0.5),
        "ret_log1m_decay": base_decay[None, None, :] + nrm(ks[5], (N_RET_LAYERS, 2, RET_HEADS), 0.1),
        "ret_w_out": nrm(ks[6], (N_RET_LAYERS, RET_V_WIDTH, D_MODEL), RET_V_WIDTH ** -0.5),
        "conv_w_in": nrm(ks[7], (N_CONV_LAYERS, D_MODEL, 2 * D_MODEL), D_MODEL ** -0.5),
        "conv_b_in": nrm(ks[8], (N_CONV_LAYERS, 2 * D_MODEL), 0.02),
        "conv_w_dw": nrm(ks[9], (N_CONV_LAYERS, CONV_WIDTH, D_MODEL), CONV_WIDTH ** -0.5),
        "conv_b_dw": nrm(ks[10], (N_CONV_LAYERS, D_MODEL), 0.02),
        "conv_ln_g": 1.0 + nrm(ks[11], (N_CONV_LAYERS, D_MODEL), 0.05),
        "conv_ln_b": nrm(ks[12], (N_CONV_LAYERS, D_MODEL), 0.02),
        "conv_w_out": nrm(ks[13], (N_CONV_LAYERS, D_MODEL, D_MODEL), D_MODEL ** -0.5),
        "conv_b_out": nrm(ks[14], (N_CONV_LAYERS, D_MODEL), 0.02),
        "attn_w_in": nrm(ks[15], (N_ATTN_LAYERS, D_MODEL, ATTN_IN_WIDTH), D_MODEL ** -0.5),
        "attn_w_out": nrm(ks[16], (N_ATTN_LAYERS, ATTN_HEADS * ATTN_HEAD_DIM, D_MODEL),
                          (ATTN_HEADS * ATTN_HEAD_DIM) ** -0.5),
    }

def second_block(x, norm_w, ffn_w_in, ffn_w_out, ret_w_in, ret_log1m_decay, ret_w_out,
              conv_w_in, conv_b_in, conv_w_dw, conv_b_dw, conv_ln_g, conv_ln_b,
              conv_w_out, conv_b_out, attn_w_in, attn_w_out):
    for i in range(DEPTH_2):
        kind, j = i % N_MIXERS, i // N_MIXERS
        hn = _rmsnorm(x, norm_w[i, 0])
        if kind == 0:
            m = _retention_mixer(hn, ret_w_in[j], ret_log1m_decay[j], ret_w_out[j])
        elif kind == 1:
            m = _conv_mixer(hn, conv_w_in[j], conv_b_in[j], conv_w_dw[j], conv_b_dw[j],
                            conv_ln_g[j], conv_ln_b[j], conv_w_out[j], conv_b_out[j])
        else:
            m = _dilated_attention_mixer(hn, attn_w_in[j], attn_w_out[j])
        x = x + _rmsnorm(m, norm_w[i, 1])
        f = _swiglu_2(_rmsnorm(x, norm_w[i, 2]), ffn_w_in[i], ffn_w_out[i])
        x = x + _rmsnorm(f, norm_w[i, 3])
    return x


def setup_inputs(seed=0):
    out = dict(first_inputs(seed))
    for name, value in second_inputs(seed + 1).items():
        if name != "x":
            out[name + "_2"] = value
    return out


def reference(
    x, c, ctx, c_ctx, ada_w, ada_b, norm1_g, norm2_g, ffn_w_gate, ffn_w_up, ffn_w_down, ev_w_in,
    ev_w_out, ev_q_norm, ev_k_norm, ev_sink, od_w_in, od_w_out, od_q_norm, od_k_norm,
    od_rel_bias, norm_w_2, ffn_w_in_2, ffn_w_out_2, ret_w_in_2, ret_log1m_decay_2, ret_w_out_2,
    conv_w_in_2, conv_b_in_2, conv_w_dw_2, conv_b_dw_2, conv_ln_g_2, conv_ln_b_2, conv_w_out_2,
    conv_b_out_2, attn_w_in_2, attn_w_out_2,
):
    x = first_block(
        x, c, ctx, c_ctx, ada_w, ada_b, norm1_g, norm2_g, ffn_w_gate, ffn_w_up, ffn_w_down,
        ev_w_in, ev_w_out, ev_q_norm, ev_k_norm, ev_sink, od_w_in, od_w_out, od_q_norm,
        od_k_norm, od_rel_bias,
    )
    return second_block(
        x, norm_w_2, ffn_w_in_2, ffn_w_out_2, ret_w_in_2, ret_log1m_decay_2, ret_w_out_2,
        conv_w_in_2, conv_b_in_2, conv_w_dw_2, conv_b_dw_2, conv_ln_g_2, conv_ln_b_2,
        conv_w_out_2, conv_b_out_2, attn_w_in_2, attn_w_out_2,
    )


_drawn_inputs = setup_inputs


def setup_inputs(seed=0):
    import zlib

    import numpy as np

    out = dict(_drawn_inputs(seed))
    spreads = {}
    factors = {'norm1_g': 6.184,
     'norm2_g': 2.845,
     'ev_q_norm': 8.0,
     'ev_k_norm': 8.0,
     'ev_sink': 8.0,
     'od_q_norm': 8.0,
     'od_k_norm': 8.0,
     'od_rel_bias': 8.0,
     'conv_b_in_2': 21.08,
     'conv_ln_b_2': 22.77,
     'conv_b_dw_2': 8.0,
     'conv_ln_g_2': 7.932,
     'conv_b_out_2': 8.0}
    for name, (base, spread) in spreads.items():
        noise = np.random.default_rng([zlib.crc32(name.encode()), seed]).standard_normal(out[name].shape)
        drawn = base * np.exp(spread * noise) if base else spread * noise
        out[name] = __import__('jax').numpy.asarray(drawn.astype(out[name].dtype))
    for name, factor in factors.items():
        out[name] = (out[name] * factor).astype(out[name].dtype)
    return out
```

```python
from contextlib import ExitStack

import numpy as np
import concourse.bass as bass
from concourse import mybir

F32 = mybir.dt.float32
F32R = mybir.dt.float32r
ALU = mybir.AluOpType
ACT = mybir.ActivationFunctionType
AX = mybir.AxisListType

P = 128
T = 256
D = 1024
C = D // P
HD = 64
FF = 2816
FC = FF // P
NA_H, NA_KH, NA_KW, GW = 16, 8, 16, 64
EPS, LN_EPS, NEG = 1e-6, 1e-5, -1e30
RET_H, RET_DK, RET_DV = 4, 256, 512
RC = RET_H * RET_DV // P
TAPS = 31
PAD = (TAPS - 1) // 2
CONV_V = 5
DIAGS = 8
RING = 3
AHEAD = 2
TW = 2048

STREAM = [("ada0", 24), ("ada1", 24), ("ev_in", 5), ("ev_out", 4), ("ffn0", 33),
          ("od_q", 4), ("od_kv", 8), ("od_out", 4), ("ffn1", 33),
          ("ret0", 24), ("ret0_out", 8), ("f0", 33), ("conv", 8), ("conv_out", 4), ("f1", 33),
          ("att", 36), ("att_out", 4), ("f2", 33), ("ret1", 24), ("ret1_out", 8), ("f3", 33)]
TILE_AT = {}
_n = 0
for _name, _k in STREAM:
    TILE_AT[_name] = _n
    _n += _k
TILES = _n
READS = [(0, TILE_AT["od_q"]),
         (TILE_AT["ev_in"], TILE_AT["od_q"] - TILE_AT["ev_in"]),
         (TILE_AT["od_kv"], 8),
         (TILE_AT["od_q"], TILES - TILE_AT["od_q"])]
NT = sum(n for _, n in READS)

PARAMS = [("c", 2 * C), ("ada_b", 2 * 48), ("norm1_g", 2 * C), ("norm2_g", 2 * C),
          ("norm_w", 4 * 4 * C), ("conv_b_in", 2 * C), ("conv_b_dw", C), ("conv_ln_g", C),
          ("conv_ln_b", C), ("conv_b_out", C), ("conv_w_dw", TAPS * C),
          ("od_q_g", 1), ("od_k_g", 1), ("ev_q_g", HD), ("ev_k_g", HD), ("sink", 8),
          ("decay", 2 * 2 * RET_H)]
PARAM_AT = {}
_n = 0
for _name, _k in PARAMS:
    PARAM_AT[_name] = (_n, _k)
    _n += _k
PARAM_W = _n

CONSTS = [("add_parts", 2), ("ident", P), ("ones", P), ("dft_c", 2 * P), ("dft_l", 4 * T), ("ev_cos", 2 * HD),
          ("ev_sin", 2 * HD), ("win_mask", 2 * 2 * T), ("na_mask", GW), ("ret_cos", T),
          ("ret_sin", T), ("dpos", 2 * T), ("dneg", 2 * T), ("dil_cos", 2 * 16),
          ("dil_sin", 2 * 16), ("dil_mask", 2 * 3 * T), ("eps", 2)]
CONST_AT = {}
_n = 0
for _name, _k in CONSTS:
    CONST_AT[_name] = (_n, _k)
    _n += _k
CONST_W = _n


def constants():
    t = np.arange(T)
    out = {}
    out["add_parts"] = np.zeros((P, 2))
    out["add_parts"][0:4] = [[1, 0], [0, 1], [1, 0], [0, 1]]
    out["ident"] = np.eye(P)
    out["ones"] = np.ones((P, P))
    ang = 2 * np.pi * np.outer(np.arange(P), np.arange(P)) / P
    out["dft_c"] = np.concatenate([np.cos(ang), np.sin(ang)], 1)
    ang = 2 * np.pi * (np.outer(t, t) % T) / T
    both = np.stack([np.cos(ang), -np.sin(ang)], 1) / np.sqrt(T * P)
    out["dft_l"] = both.reshape(2, P, 2, T).transpose(1, 0, 2, 3)
    inv = (np.float32(10000.0) ** (-np.arange(16, dtype=np.float32) / np.float32(16))).astype(np.float32)
    row, col = (t // GW).astype(np.float32), (t % GW).astype(np.float32)
    ar, ac = (row[:, None] * inv).astype(np.float64), (col[:, None] * inv).astype(np.float64)
    cos = np.concatenate([np.cos(ar), np.cos(ar), np.cos(ac), np.cos(ac)], 1)
    sin = np.concatenate([-np.sin(ar), np.sin(ar), -np.sin(ac), np.sin(ac)], 1)
    tok = lambda a: a.reshape(2, P, -1).transpose(1, 0, 2)
    out["ev_cos"], out["ev_sin"] = tok(cos), tok(sin)
    mask = np.where(np.abs(t[:, None] - t[None, :]) <= 128, 0.0, NEG)
    out["win_mask"] = tok(np.concatenate([mask, np.zeros((T, T))], 1))
    cq = np.arange(GW)
    c0 = np.clip(cq - NA_KW // 2, 0, GW - NA_KW)
    ok = (cq[None, :] >= c0[:, None]) & (cq[None, :] < c0[:, None] + NA_KW)
    out["na_mask"] = np.where(ok, 0.0, NEG)[np.arange(P) % GW]
    lin = np.linspace(0.0, 1.0, RET_DK // 2, dtype=np.float32)
    inv = (np.float32(1.0) / (np.float32(10000.0) ** lin)).astype(np.float32)
    ang = (t.astype(np.float32)[:, None] * inv).astype(np.float64).T
    out["ret_cos"], out["ret_sin"] = np.cos(ang), np.sin(ang)
    diff = t[None, :] - t[:, None]
    out["dpos"], out["dneg"] = tok(np.maximum(diff, 0)), tok(np.maximum(-diff, 0))
    inv = (np.float32(500000.0) ** (-np.arange(0, 16, 2, dtype=np.float32) / np.float32(16))).astype(np.float32)
    ang = (t.astype(np.float32)[:, None] * inv).astype(np.float64)
    out["dil_cos"] = tok(np.concatenate([np.cos(ang), np.cos(ang)], 1))
    out["dil_sin"] = tok(np.concatenate([-np.sin(ang), np.sin(ang)], 1))
    d = t[:, None] - t[None, :]
    ms = [np.where(np.abs(d) <= 64, 0.0, NEG), np.where(d % 4 == 0, 0.0, NEG),
          np.where(d % 16 == 0, 0.0, NEG)]
    out["dil_mask"] = tok(np.concatenate(ms, 1))
    out["eps"] = np.tile(np.array([[EPS, LN_EPS]]), (P, 1))
    return np.ascontiguousarray(np.concatenate(
        [out[n].reshape(P, -1) for n, _ in CONSTS], 1).astype(np.float32))


def make_plan():
    plan = []
    at = dict(t=0, n=0, b=0, u=0, f=0, q=0, ot=0, xu=0, fo=0, ea=0, ed=0, ada=0, rt=0, m=0)

    def add(kind, **kw):
        ph = dict(kind=kind, at=dict(at), **kw)
        plan.append(ph)
        return ph

    def norm(src, how, **kw):
        add("norm", src=src, how=how, **kw)
        at["n"] += 1
        if how == "post":
            at["xu"] += C

    def gemm_b(src, chunks, evac, **kw):
        add("gemm_b", src=src, chunks=chunks, evac=evac, **kw)
        at["t"] += chunks // 2
        at["b"] += 1
        if evac == "gate":
            at["xu"] += C
        else:
            at["m"] += C

    def ffn():
        add("ffn_a")
        at["t"] += FC
        at["ed"] += FC
        at["f"] += FC

    def qkv(tiles, **kw):
        add("qkv", tiles=tiles, **kw)
        at["t"] += len(tiles)
        at["q"] += sum(k in "qk" for k, *_ in tiles)
        at["ea"] += sum(k in "vf" or kw["which"] == "dil" for k, *_ in tiles)

    def attend(which, units, **kw):
        add("attend", which=which, units=units, **kw)
        at["u"] += units
        at["ot"] += kw["banks"]

    add("setup")
    for l in range(2):
        add("ada", l=l)
        at["t"] += 24
        at["ada"] += 1
    for who in ("ctx", "lat"):
        norm(who, "ada", l=0, which=0)
        qkv([("f", 0), ("f", 1), ("q", 0), ("q", 1), ("k", 0)], which="ev", who=who)
        add("fourier")
        at["fo"] += 4
        attend("ev", 16, who=who, banks=2)
        gemm_b("H", 8, "gate", who=who, l=0, g=2)
        norm(who, "ada", l=0, which=1)
        ffn()
        gemm_b("A", FC, "gate", who=who, l=0, g=5)
    norm("ctx", "ada", l=1, which=0)
    qkv([("k", i) for i in range(4)] + [("v", i) for i in range(4)], which="od", who="ctx")
    norm("lat", "ada", l=1, which=0)
    qkv([("q", i) for i in range(4)] + [("k", i) for i in range(4)] + [("v", i) for i in range(4)],
        which="od", who="lat")
    attend("od", 32, who="lat", banks=4)
    gemm_b("H", 8, "gate", who="lat", l=1, g=2)
    norm("lat", "ada", l=1, which=1)
    ffn()
    gemm_b("A", FC, "gate", who="lat", l=1, g=5)
    for i in range(4):
        norm("lat", "pre", w=4 * i)
        if i in (0, 3):
            add("ret", r=i // 3)
            at["t"] += 24
            at["ed"] += 8
            at["ea"] += 16
            at["rt"] += 1
            gemm_b("A", RC, "m")
        elif i == 1:
            add("conv")
            at["t"] += 8
            at["ed"] += 8
            gemm_b("H", 8, "mb")
        else:
            for half in range(2):
                qkv([(k, g) + (j,) for g in range(3) for k in "qkv" for j in range(2)],
                    which="dil", who="lat")
                attend("dil", 16, who="lat", banks=2, half=half)
            gemm_b("S", 8, "m")
        norm("M", "post", w=4 * i + 1)
        norm("lat", "pre", w=4 * i + 2)
        ffn()
        gemm_b("A", FC, "m")
        norm("M", "post", w=4 * i + 3)
    plan.append(dict(kind="end", at=dict(at)))
    assert at["t"] == NT, (at["t"], NT)
    return plan


def two_blocks_kernel(nc, weights, x_in, ctx_in, params_in, consts_in, rel_bias, out):
    plan = make_plan()
    with ExitStack() as ctx:
        def sb(name, shape, dt=F32):
            return ctx.enter_context(nc.sbuf_tensor(name, shape, dt))

        def sem(name):
            return ctx.enter_context(nc.semaphore(name))

        w_raw = sb("w_raw", [P, RING, TW])
        w_hi = sb("w_hi", [P, RING, TW], F32R)
        w_lo = sb("w_lo", [P, RING, TW], F32R)
        X = sb("X", [P, C, T])
        Y = sb("Y", [P, C, T])
        M = Y
        H_hi = sb("H_hi", [P, C, T], F32R)
        H_lo = sb("H_lo", [P, C, T], F32R)
        consts = sb("consts", [P, CONST_W])
        params = sb("params", [P, PARAM_W])
        mod = sb("mod", [P, 2, 48, 2])
        mod_g = sb("mod_g", [P, 2, 2, C, 2])
        c_silu = sb("c_silu", [P, C, 2])
        rstd = sb("rstd", [P, T])
        small = sb("small", [P, 4, 8])
        od_q_gain = sb("od_q_gain", [P, 1])
        dil_t = sb("dil_t", [P, 2, 2 * 4 * 16])
        head_sum = sb("head_sum", [P, 8])
        head_std = sb("head_std", [P, 8])
        head_inv = sb("head_inv", [P, 8])
        unread = sb("unread", [P, 32])
        tok_std = sb("tok_std", [P, 2])
        tok_inv = sb("tok_inv", [P, 2])
        decay = sb("decay", [P, 2 * 2 * RET_H])
        ev_kc = sb("ev_kc", [P, 2, T])
        ev_vc = sb("ev_vc", [P, 2, P])
        ARENA = 70 * 1024
        base = -(-nc.sbuf_base // 32) * 32
        sb("arena", [P, ARENA // 4 + 8])

        def over(name, at_kib, shape, dt=F32):
            words = int(np.prod(shape[1:]))
            assert at_kib * 1024 + 4 * words <= ARENA, name
            return nc.alloc_sbuf_tensor_at(name, shape, dt, offset=base + at_kib * 1024)

        c_wide = over("c_wide", 0, [P, C, P], F32R)
        ada_rows = over("ada_rows", 8, [4, RING, 256])
        diag = over("diag", 59, [P, 2, P])
        A_hi = over("A_hi", 0, [P, FC, T], F32R)
        A_lo = over("A_lo", 22, [P, FC, T], F32R)
        sq = over("sq", 61, [P, C, T])
        sil = over("sil", 61, [P, 3, 2 * T])
        a32 = over("a32", 67, [P, 3, T])
        qT = over("qT", 0, [P, C, T])
        kT = over("kT", 8, [P, C, T])
        v = over("v", 16, [P, 2, D])
        kcT = over("kcT", 24, [P, C, T])
        vc = over("vc", 32, [P, 2, D])
        O = over("O", 40, [P, 2, D])
        ev_k = over("ev_k", 8, [P, 2, T])
        ev_v = over("ev_v", 10, [P, 2, P])
        fT = over("fT", 12, [P, 4, T])
        fab = over("fab", 16, [P, 2, 2, T])
        stage = over("stage", 48, [P, 3, 2 * T])
        head_sq = over("head_sq", 54, [P, 2 * T])
        bias = over("bias", 56, [P, 4, 6 * GW])
        bias_raw = [over("bias_raw0", 54, [P, 6 * GW]), over("bias_raw1", 68, [P, 6 * GW])]
        prob_a = over("prob", 48, [P, 2, 3 * T])
        probT = over("probT", 62, [P, 2, 3 * T])
        rope_t = over("rope_t", 62, [P, 2, 2 * T])
        dq = over("dq", 0, [P, 12, T])
        dk = over("dk", 12, [P, 12, T])
        dv = over("dv", 24, [P, 3, 2, 2 * T])
        dO = over("dO", 36, [P, 2, 2 * T])
        S_hi = over("S_hi", 40, [P, C, T], F32R)
        S_lo = over("S_lo", 48, [P, C, T], F32R)
        dstage = over("dstage", 56, [P, 3, 2 * T])
        prob_d = over("prob_d", 56, [P, 2, 3 * T])
        rq = over("rq", 0, [P, C, T])
        rk = over("rk", 8, [P, C, T])
        rv = over("rv", 16, [P, 2, RET_H * RET_DV])
        ro = over("ro", 45, [P, RC, T])
        rD = over("rD", 61, [P, RET_H, 2, T])
        rst = over("rst", 42, [P, 2, T])
        rarg = over("rarg", 40, [P, 2, T])
        rtmp = over("rtmp", 53, [P, 2, 2 * T])
        rsq = over("rsq", 32, [P, 2, 4, T])
        upad = over("upad", 0, [P, C, T + 2 * PAD])
        cv = over("cv", 10, [P, C, T])
        taps_diag = over("taps_diag", 18, [P, DIAGS, P])

        ps = ctx.enter_context(nc.psum_tensor("ps", [P, 8, 512], F32))

        loaded = [sem(f"loaded{i}") for i in range(RING)]
        hi_done = sem("hi_done")
        lo_done = sem("lo_done")
        tile_done = sem("tile_done")
        a_evac = sem("a_evac")
        v_evac = sem("v_evac")
        ada_evac = sem("ada_evac")
        inputs = sem("inputs")
        stored = sem("stored")
        act_c = sem("act_c")
        dve_c = sem("dve_c")
        pool_c = sem("pool_c")
        ada_done = sem("ada_done")
        c_zeroed = sem("c_zeroed")
        c_rounded = sem("c_rounded")
        ada_mm = sem("ada_mm")
        ada_row = sem("ada_row")
        n_diag = sem("n_diag")
        n_bcast = sem("n_bcast")
        setup_done = sem("setup_done")
        n_sq = sem("n_sq")
        n_sum = sem("n_sum")
        n_std = sem("n_std")
        n_t = sem("n_t")
        n_hi = sem("n_hi")
        n_lo = sem("n_lo")
        b_done = sem("b_done")
        x_up = sem("x_up")
        m_evac = sem("m_evac")
        f_sil = sem("f_sil")
        f_hi = sem("f_hi")
        f_split = sem("f_split")
        q_sq = sem("q_sq")
        q_ss = sem("q_ss")
        q_std = sem("q_std")
        q_staged = sem("q_staged")
        q_turned = sem("q_turned")
        q_evac = sem("q_evac")
        fo_ab = sem("fo_ab")
        fo_cp = sem("fo_cp")
        fo_mix = sem("fo_mix")
        fo_hi = sem("fo_hi")
        fo_lo = sem("fo_lo")
        s_done = sem("s_done")
        s_max = sem("s_max")
        p_exp = sem("p_exp")
        pt_done = sem("pt_done")
        pt_copy = sem("pt_copy")
        o_done = sem("o_done")
        o_evac = sem("o_evac")
        ot_done = sem("ot_done")
        ot_hi = sem("ot_hi")
        ot_lo = sem("ot_lo")
        b_loaded = [sem(f"b_loaded{i}") for i in range(2)]
        b_masked = sem("b_masked")
        r_arg = sem("r_arg")
        r_D = sem("r_D")
        r_rope = sem("r_rope")
        r_s = sem("r_s")
        r_st = sem("r_st")
        r_o = sem("r_o")
        r_cp = sem("r_cp")
        r_sum = sem("r_sum")
        r_std = sem("r_std")
        r_on = sem("r_on")
        r_gate = sem("r_gate")
        r_split = sem("r_split")
        r_lg = sem("r_lg")
        c_conv = sem("c_conv")
        c_mean = sem("c_mean")
        c_dev = sem("c_dev")
        c_sq = sem("c_sq")
        c_var = sem("c_var")
        c_std = sem("c_std")
        c_t = sem("c_t")
        c_y = sem("c_y")
        c_lo = sem("c_lo_done")
        c_sg = sem("c_sg")
        padded = sem("padded")
        taps = sem("taps")
        diag_made = sem("diag_made")
        diag_used = sem("diag_used")
        c_tensor = sem("c_tensor")

        def con(name, *dims):
            a, n = CONST_AT[name]
            return consts[:, a:a + n]

        def par(name, i=0, n=1):
            a, _ = PARAM_AT[name]
            return params[:, a + i:a + i + n]

        ident, ones = con("ident"), con("ones")
        dft_l = con("dft_l").rearrange("p (b r t) -> p b r t", b=2, r=2)
        win_mask = con("win_mask").rearrange("p (b k) -> p b k", b=2)
        dil_mask = con("dil_mask").rearrange("p (b k) -> p b k", b=2)
        eps, ln_eps = consts[:, CONST_AT["eps"][0]:CONST_AT["eps"][0] + 1], \
            consts[:, CONST_AT["eps"][0] + 1:CONST_AT["eps"][0] + 2]
        res = {"lat": X, "ctx": Y, "M": M}
        col = {"lat": 0, "ctx": 1}
        src_of = {"H": (H_hi, H_lo), "A": (A_hi, A_lo), "S": (S_hi, S_lo)}

        def whole(t):
            return t.bitcast(F32)

        def in_loop(eng, n, step):
            full = n // RING if n >= 2 * RING else 0
            if full:
                with eng.Fori(0, full) as i:
                    for j in range(RING):
                        step(i, j)
            for o in range(full * RING, n):
                step(o // RING, o % RING)

        block = ctx.enter_context(nc.Block())

        @block.sync
        def _(sp):
            sp.dma_start(params[:], params_in).then_inc(inputs, 16)
            sp.dma_start(consts[:], consts_in).then_inc(inputs, 16)
            sp.dma_start(Y[:], ctx_in).then_inc(inputs, 16)
            sp.dma_start(X[:], x_in).then_inc(inputs, 16)
            t0 = 0
            for first, n in READS:
                def load(i, j):
                    slot = (t0 + j) % RING
                    tile = t0 + RING * i + j
                    if not isinstance(tile, int) or tile >= RING:
                        sp.wait_ge(lo_done, tile - RING + 1)
                    src = weights[bass.ds(first + RING * i + j, 1)].rearrange("a p w -> (a p) w")
                    sp.dma_start(w_raw[:, slot, :], src).then_inc(loaded[slot], 16)
                if t0 == 0:
                    for j in range(RING):
                        load(0, j)
                    t0, first, n = RING, first + RING, n - RING
                in_loop(sp, n, load)
                t0 += n
            sp.wait_ge(x_up, plan[-1]["at"]["xu"])
            sp.dma_start(out, X[:]).then_inc(stored, 16)
            sp.wait_ge(stored, 16)

        @block.tensor
        def _(pe):
            mm = nc.tensor.matmul

            def tile_ready(ph, i, j):
                pe.wait_ge(lo_done, ph["at"]["t"] + RING * i + j + 1)

            def three(out, whi, wlo, k, cols, hi, lo, first, last):
                mm(out, whi[:, cols], hi, start=first, stop=False, skip_group_check=True)
                mm(out, whi[:, cols], lo, start=False, stop=False, skip_group_check=True)
                return mm(out, wlo[:, cols], hi, start=False, stop=last, skip_group_check=True)

            def a_feature(slot, banks, hi, lo, n=T):
                for c in range(2):
                    for k in range(C):
                        cols = slice(k * 256 + c * P, k * 256 + c * P + P)
                        last = three(banks[c], w_hi[:, slot, :], w_lo[:, slot, :], k, cols,
                                     hi[:, k, :], lo[:, k, :], k == 0, k == C - 1)
                return last

            def a_token(slot, hi, lo):
                for b in range(2):
                    bank = ps[:, 2 * slot + b, 0:T]
                    tok = slice(b * P, b * P + P)
                    for k in range(C):
                        cols = slice(k * 256, k * 256 + 256)
                        mm(bank, hi[:, k, tok], w_hi[:, slot, cols], start=k == 0, stop=False)
                        mm(bank, hi[:, k, tok], w_lo[:, slot, cols], start=False, stop=False)
                        last = mm(bank, lo[:, k, tok], w_hi[:, slot, cols], start=False, stop=k == C - 1)
                return last

            def ada(ph):
                pe.wait_ge(setup_done, 1)

                def step(i, j):
                    at = ph["at"]["t"] + RING * i + j
                    slot = (ph["at"]["t"] + j) % RING
                    tile_ready(ph, i, j)
                    pe.wait_ge(ada_evac, at + 1)
                    for k in range(C):
                        for part in (w_hi, w_lo):
                            last = mm(ps[:, slot, 0:256], c_wide[:, k, :], part[:, slot, k * 256:k * 256 + 256],
                                      start=k == 0 and part is w_hi, stop=k == C - 1 and part is w_lo)
                    last.then_inc(ada_mm, 1)
                    pe.wait_ge(ada_row, at + 1)
                    for c in range(2):
                        last = mm(ps[:, 3 + slot, 2 * c:2 * c + 2], ada_rows[:, slot, c * P:c * P + P],
                                  con("add_parts")[0:4, :], start=True, stop=True)
                    last.then_inc(tile_done, 1)
                in_loop(pe, 24, step)

            def norm(ph):
                n = ph["at"]["n"]
                before = plan[plan.index(ph) - 1]["kind"]
                if before == "ada":
                    pe.wait_ge(ada_done, 2)
                if before == "qkv":
                    pe.wait_ge(q_staged, ph["at"]["q"])
                    pe.wait_ge(v_evac, RING + ph["at"]["ea"])
                for c in range(C):
                    pe.wait_ge(n_sq, C * n + c + 1)
                    for b in range(2):
                        last = mm(ps[:, 0, b:b + 1], sq[:, c, b * P:b * P + P], ones[:, 0:1],
                                  start=c + b == 0, stop=c == C - 1, skip_group_check=True)
                last.then_inc(n_sum, 1)
                pe.wait_ge(n_diag, n + 1)
                mm(ps[:, 1, 0:T], ones, diag[:].rearrange("p b t -> p (b t)"), start=True,
                   stop=True).then_inc(n_bcast, 1)

            def wait_h(ph):
                pe.wait_ge(n_lo, C * sum(p["kind"] == "norm" and p["how"] != "post"
                                         for p in plan[:plan.index(ph)]))

            def slot_read(ph, j):
                if j < RING:
                    return
                at, o = ph["at"], j - RING
                if ph["kind"] == "qkv":
                    kinds = [k for k, *_ in ph["tiles"][:o + 1]]
                    if ph["which"] == "dil":
                        pe.wait_ge(v_evac, RING + at["ea"] + o + 1)
                    elif kinds[-1] in "qk":
                        pe.wait_ge(q_staged, at["q"] + sum(k in "qk" for k in kinds))
                    else:
                        pe.wait_ge(v_evac, RING + at["ea"] + sum(k in "vf" for k in kinds))
                elif ph["kind"] == "ret" and o >= 8:
                    pe.wait_ge(v_evac, RING + at["ea"] + o - 8 + 1)
                else:
                    pe.wait_ge(a_evac, RING + at["ed"] + o + 1)

            def turn(ph, q, src):
                pe.wait_ge(q_staged, q + 1)
                if q >= 2:
                    pe.wait_ge(q_evac, q - 1)
                for c in range(2):
                    for b in range(2):
                        last = nc.tensor.transpose(ps[:, 6 + q % 2, (2 * c + b) * P:(2 * c + b + 1) * P],
                                                   src[:, b * 256 + c * P:b * 256 + c * P + P], ident)
                last.then_inc(q_turned, 1)

            def qkv(ph):
                wait_h(ph)
                if plan[plan.index(ph) - 1]["kind"] == "attend":
                    pe.wait_ge(ot_lo, ph["at"]["ot"])
                staging = dstage if ph["which"] == "dil" else stage
                q = ph["at"]["q"]
                waiting = None
                for j, (kind, *_) in enumerate(ph["tiles"]):
                    slot = (ph["at"]["t"] + j) % RING
                    tile_ready(ph, 0, j)
                    slot_read(ph, j)
                    if kind == "f":
                        last = a_feature(slot, [ps[:, 2 * slot, 0:T], ps[:, 2 * slot + 1, 0:T]], H_hi, H_lo)
                    else:
                        last = a_token(slot, H_hi, H_lo)
                    last.then_inc(tile_done, 1)
                    if waiting is not None:
                        turn(ph, *waiting)
                        waiting = None
                    if kind in "qk":
                        waiting = (q, staging[:, slot, :])
                        q += 1
                if waiting is not None:
                    turn(ph, *waiting)

            def fourier(ph):
                f = ph["at"]["fo"]
                pe.wait_ge(v_evac, RING + ph["at"]["ea"])
                pe.wait_ge(q_staged, ph["at"]["q"])
                for g in range(5):
                    if g < 4:
                        if g >= 2:
                            pe.wait_ge(fo_cp, f + g - 1)
                        for b in range(2):
                            last = mm(ps[:, g % 2, b * T:b * T + T], fT[:, g, b * P:b * P + P],
                                      con("dft_c"), start=True, stop=True)
                        last.then_inc(fo_ab, 1)
                    if g >= 1:
                        h = g - 1
                        pe.wait_ge(fo_cp, f + h + 1)
                        if h >= 2:
                            pe.wait_ge(fo_lo, f + h - 1)
                        for b in range(2):
                            for r in range(2):
                                last = mm(ps[:, 2 + h % 2, 0:T], fab[:, h % 2, b, r * P:r * P + P],
                                          dft_l[:, b, r, :], start=b + r == 0, stop=b + r == 2)
                        last.then_inc(fo_mix, 1)

            def attend(ph):
                u0, n, which = ph["at"]["u"], ph["units"], ph["which"]
                prob = prob_d if which == "dil" else prob_a
                pe.wait_ge(q_evac, ph["at"]["q"])
                pe.wait_ge(v_evac, RING + ph["at"]["ea"])
                if which == "ev":
                    pe.wait_ge(fo_lo, ph["at"]["fo"])
                pe.wait_ge(q_staged, ph["at"]["q"])
                lat = ph["who"] == "lat"

                def scores(u):
                    h, b = u // 2, u % 2
                    bank = 2 * (u % 2)
                    if u >= 2:
                        pe.wait_ge(s_max, u0 + u - 1)
                    rows = slice(64 * (h % 2), 64 * (h % 2) + 64)
                    tok = slice(b * P, b * P + P)
                    if which == "ev":
                        kv = h // 4
                        ks = [ev_k[rows, kv, :], ev_kc[rows, kv, :]] if lat else [ev_kc[rows, kv, :]]
                        q = qT[rows, h // 2, tok]
                        lhs = [q] * len(ks)
                    elif which == "od":
                        ks = [kT[rows, h // 2, :], kcT[rows, h // 2, :]]
                        lhs = [qT[rows, h // 2, tok]] * 2
                    else:
                        ks = [dk[rows, 4 * g + h // 2, :] for g in range(3)]
                        lhs = [dq[rows, 4 * g + h // 2, tok] for g in range(3)]
                    for g, k in enumerate(ks):
                        last = mm(ps[:, bank + g // 2, (g % 2) * T:(g % 2) * T + T], lhs[g], k,
                                  start=True, stop=True)
                    last.then_inc(s_done, 1)

                blocks = {"ev": 4 if lat else 2, "od": 4, "dil": 6}[which]

                def turn_p(u):
                    pe.wait_ge(p_exp, u0 + u + 1)
                    if u >= 1:
                        pe.wait_ge(pt_copy, u0 + u)
                    for k in range(blocks):
                        last = nc.tensor.transpose(ps[:, 4 + k // 4, (k % 4) * P:(k % 4) * P + P],
                                                   prob[:, u % 2, k * P:k * P + P], ident)
                    last.then_inc(pt_done, 1)

                def weigh(u):
                    h = u // 2
                    pe.wait_ge(pt_copy, u0 + u + 1)
                    if u >= 2:
                        pe.wait_ge(o_evac, u0 + u - 1)
                    for k in range(blocks):
                        b = k % 2
                        if which == "ev":
                            vv = ev_v if lat and k < 2 else ev_vc
                            val = vv[:, b, 64 * (h // 4):64 * (h // 4) + 64]
                        elif which == "od":
                            val = (v if k < 2 else vc)[:, b, 64 * h:64 * h + 64]
                        else:
                            val = dv[:, k // 2, b, 64 * h:64 * h + 64]
                        last = mm(ps[:, 6 + u % 2, 0:64], probT[:, u % 2, k * P:k * P + P], val,
                                  start=k == 0, stop=k == blocks - 1)
                    last.then_inc(o_done, 1)

                for i in range(n + 2):
                    if i < n:
                        scores(i)
                    if 1 <= i <= n:
                        turn_p(i - 1)
                    if i >= 2:
                        weigh(i - 2)
                pe.wait_ge(o_evac, u0 + n)
                outs = dO if which == "dil" else O
                for k in range(ph["banks"]):
                    for c in range(2):
                        for b in range(2):
                            last = nc.tensor.transpose(
                                ps[:, k, (2 * c + b) * P:(2 * c + b + 1) * P],
                                outs[:, b, (2 * k + c) * P:(2 * k + c + 1) * P], ident)
                    last.then_inc(ot_done, 1)

            def gemm_b(ph):
                hi, lo = src_of[ph["src"]]
                n = ph["chunks"] // 2
                at = ph["at"]
                prev = plan[plan.index(ph) - 1]
                if prev["kind"] == "attend":
                    pe.wait_ge(ot_lo, at["ot"])
                elif prev["kind"] == "ffn_a":
                    pe.wait_ge(f_split, at["f"] + RING)
                elif prev["kind"] == "ret":
                    pe.wait_ge(r_split, 8 * at["rt"])
                else:
                    pe.wait_ge(c_lo, C)

                def tile(i, j, o, first=False, final=False):
                    slot = (at["t"] + j) % RING
                    tile_ready(ph, i, j)
                    for c in range(C):
                        for k in range(2):
                            cols = slice(k * D + c * P, k * D + c * P + P)
                            if isinstance(o, int):
                                h, l = hi[:, 2 * o + k, :], lo[:, 2 * o + k, :]
                            else:
                                h = hi[:, bass.ds(2 * o + k, 1), :].rearrange("p a t -> p (a t)")
                                l = lo[:, bass.ds(2 * o + k, 1), :].rearrange("p a t -> p (a t)")
                            last = three(ps[:, c, 0:T], w_hi[:, slot, :], w_lo[:, slot, :], k, cols,
                                         h, l, first and k == 0, final and k == 1)
                        if final and c < C - 1:
                            last.then_inc(b_done, 1)
                    last.then_inc(tile_done, 1)

                tile(0, 0, 0, first=True)
                body = (n - 2) // RING
                o = 1
                if body >= 2:
                    with pe.Fori(0, body) as i:
                        for j in range(RING):
                            tile(i, 1 + j, RING * i + 1 + j)
                    o += body * RING
                while o < n:
                    tile(0, o, o, final=o == n - 1)
                    o += 1

            def ffn_a(ph):
                wait_h(ph)

                def step(i, j):
                    slot = (ph["at"]["t"] + j) % RING
                    tile_ready(ph, i, j)
                    pe.wait_ge(a_evac, ph["at"]["ed"] + RING * i + j + 1)
                    a_feature(slot, [ps[:, 2 * slot, 0:T], ps[:, 2 * slot + 1, 0:T]],
                              H_hi, H_lo).then_inc(tile_done, 1)
                in_loop(pe, FC, step)

            def ret(ph):
                wait_h(ph)
                at, r = ph["at"], ph["at"]["rt"]

                def project(j, feature):
                    slot = (at["t"] + j) % RING
                    tile_ready(ph, 0, j)
                    slot_read(ph, j)
                    if feature:
                        last = a_feature(slot, [ps[:, 2 * slot, 0:T], ps[:, 2 * slot + 1, 0:T]], H_hi, H_lo)
                    else:
                        last = a_token(slot, H_hi, H_lo)
                    last.then_inc(tile_done, 1)

                for j in range(16):
                    project(j, j < 8)
                pe.wait_ge(r_rope, 8 * (r + 1))
                pe.wait_ge(v_evac, at["ea"] + 8 + RING)
                for i in range(RET_H + 2):
                    if i < RET_H:
                        h = i
                        if h >= 1:
                            pe.wait_ge(r_st, RET_H * r + h)
                        for b in range(2):
                            for c in range(2):
                                last = mm(ps[:, b, 0:T], rk[:, 2 * h + c, b * P:b * P + P],
                                          rq[:, 2 * h + c, :], start=c == 0, stop=c == 1)
                        last.then_inc(r_s, 1)
                    if 1 <= i <= RET_H:
                        h = i - 1
                        pe.wait_ge(r_st, RET_H * r + h + 1)
                        if h >= 2:
                            pe.wait_ge(r_cp, 2 * (RET_H * r + h - 1))
                        for e in range(4):
                            bank, off = 4 + 2 * (h % 2) + e // 2, (e % 2) * T
                            for b in range(2):
                                last = mm(ps[:, bank, off:off + T],
                                          rv[:, b, h * RET_DV + e * P:h * RET_DV + e * P + P],
                                          rst[:, b, :], start=b == 0, stop=b == 1)
                        last.then_inc(r_o, 1)
                    if i >= 2:
                        h = i - 2
                        pe.wait_ge(r_cp, 2 * (RET_H * r + h) + 2)
                        if h >= 2:
                            pe.wait_ge(r_std, RET_H * r + h - 1)
                        for e in range(4):
                            last = mm(ps[:, 2 + h % 2, 0:T], ones, rsq[:, h % 2, e, :],
                                      start=e == 0, stop=e == 3)
                        last.then_inc(r_sum, 1)
                pe.wait_ge(r_std, RET_H * (r + 1))
                pe.wait_ge(r_cp, 2 * RET_H * (r + 1))
                for j in range(16, 24):
                    project(j, True)

            def conv(ph):
                wait_h(ph)
                at = ph["at"]
                for j in range(8):
                    slot = (at["t"] + j) % RING
                    tile_ready(ph, 0, j)
                    slot_read(ph, j)
                    a_feature(slot, [ps[:, 2 * slot, 0:T], ps[:, 2 * slot + 1, 0:T]],
                              H_hi, H_lo).then_inc(tile_done, 1)
                pe.wait_ge(a_evac, RING + at["ed"] + 8)
                pe.wait_ge(padded, 1)
                for c in range(CONV_V, C):
                    for k in range(TAPS):
                        n = (c - CONV_V) * TAPS + k
                        pe.wait_ge(diag_made, n + 1)
                        ins = mm(ps[:, c - CONV_V, 0:T], taps_diag[:, n % DIAGS, :], upad[:, c, k:k + T],
                                 start=k == 0, stop=k == TAPS - 1)
                        ins.then_inc(diag_used, 1)
                pe.wait_ge(c_tensor, C - CONV_V)
                for c in range(C):
                    if c < CONV_V:
                        pe.wait_ge(c_conv, c + 1)
                    last = mm(ps[:, 6, 0:T], ones, cv[:, c, :], start=c == 0, stop=c == C - 1)
                last.then_inc(c_mean, 1)
                for c in range(C):
                    pe.wait_ge(c_sq, c + 1)
                    last = mm(ps[:, 7, 0:T], ones, sq[:, c, :], start=c == 0, stop=c == C - 1)
                last.then_inc(c_var, 1)

            pe.sem_inc(tile_done, 1)
            for ph in plan:
                {"ada": ada, "norm": norm, "qkv": qkv, "fourier": fourier, "attend": attend,
                 "gemm_b": gemm_b, "ffn_a": ffn_a, "ret": ret, "conv": conv}.get(
                     ph["kind"], lambda _: None)(ph)

        @block.scalar
        def _(act):
            act_n = [0]

            def link(ins):
                act_n[0] += 1
                ins.then_inc(act_c, 1)
                act.wait_ge(act_c, act_n[0])

            def A(*a, **k):
                return nc.scalar.activation(*a, **k)

            def split(ph, i, j):
                t0 = ph["at"]["t"] + AHEAD
                tile = t0 + RING * i + j
                if isinstance(tile, int) and tile >= NT:
                    return
                slot = (t0 + j) % RING
                act.wait_ge(loaded[slot], ((t0 + j) // RING + i + 1) * 16)
                act.wait_ge(tile_done, tile - 1)
                A(w_hi[:, slot, :], w_raw[:, slot, :], ACT.Copy).then_inc(hi_done, 1)

            def products(ph, i, j):
                act.wait_ge(tile_done, ph["at"]["t"] + RING * i + j + 2)

            def setup(ph):
                act.sem_inc(v_evac, RING)
                act.wait_ge(inputs, 64)
                link(A(od_q_gain[:], par("od_q_g"), ACT.Copy, scale=HD ** -0.5))
                link(A(c_silu[:], par("c", 0, 2 * C).rearrange("p (c w) -> p c w", w=2), ACT.Silu))
                act.wait_ge(c_zeroed, 1)
                A(c_wide[:, :, 0:2], c_silu[:], ACT.Copy).then_inc(c_rounded, 1)
                link(A(decay[:], par("decay", 0, 16), ACT.Exp))
                link(A(decay[:], decay[:], ACT.Identity, scale=-1.0, bias=1.0))
                A(decay[:], decay[:], ACT.Ln).then_inc(r_lg, 1)
                for tile in range(AHEAD):
                    act.wait_ge(loaded[tile], 16)
                    A(w_hi[:, tile, :], w_raw[:, tile, :], ACT.Copy).then_inc(hi_done, 1)

            def ada(ph):
                def step(i, j):
                    slot = (ph["at"]["t"] + j) % RING
                    split(ph, i, j)
                    act.wait_ge(ada_mm, ph["at"]["t"] + RING * i + j + 1)
                    A(ada_rows[:, slot, :], ps[0:4, slot, 0:256], ACT.Copy).then_inc(ada_row, 1)
                in_loop(act, 24, step)

            def norm(ph):
                n, src = ph["at"]["n"], res[ph["src"]]
                A(unread[:, n:n + 1], eps, ACT.Sqrt)
                for c in range(C):
                    if ph["src"] == "M":
                        act.wait_ge(m_evac, ph["at"]["m"] - C + c + 1)
                    elif ph["at"]["xu"]:
                        act.wait_ge(x_up, ph["at"]["xu"] - C + c + 1)
                    A(sq[:, c, :], src[:, c, :], ACT.Square).then_inc(n_sq, 1)
                act.wait_ge(n_sum, n + 1)
                A(tok_std[:], ps[:, 0, 0:2], ACT.Sqrt, scale=1.0 / D, bias=eps).then_inc(n_std, 1)
                if ph["how"] == "post":
                    return
                if ph["how"] == "ada":
                    act.wait_ge(ada_done, 2)
                for c in range(C):
                    act.wait_ge(n_t, 4 * n + c // 2 + 1)
                    if ph["how"] == "ada":
                        w, l, which = col[ph["src"]], ph["l"], ph["which"]
                        A(H_hi[:, c, :], sq[:, c, :], ACT.Identity, scale=mod_g[:, l, which, c, w:w + 1],
                          bias=mod[:, l, 24 * which + c, w:w + 1]).then_inc(n_hi, 1)
                    else:
                        A(H_hi[:, c, :], sq[:, c, :], ACT.Copy,
                          scale=par("norm_w", ph["w"] * C + c)).then_inc(n_hi, 1)

            def qkv(ph):
                at, which, who = ph["at"], ph["which"], ph["who"]
                q = at["q"]
                staging = dstage if which == "dil" else stage
                normed = which != "dil"
                waiting = None

                def evac(q, tile):
                    act.wait_ge(q_turned, q + 1)
                    kind, g, *j = tile
                    for c in range(2):
                        src = ps[:, 6 + q % 2, c * T:c * T + T]
                        if which == "ev" and kind == "k":
                            dst = (ev_k if who == "lat" else ev_kc)[:, c, :]
                            ins = A(dst, src, ACT.Copy)
                        elif which == "ev":
                            ins = A(qT[:, 2 * g + c, :], src, ACT.Copy, scale=0.125)
                        elif which == "od":
                            dst = (qT if kind == "q" else kT if who == "lat" else kcT)[:, 2 * g + c, :]
                            ins = A(dst, src, ACT.Copy, scale=od_q_gain[:] if kind == "q" else par("od_k_g"))
                        else:
                            ins = A((dq if kind == "q" else dk)[:, 4 * g + 2 * j[0] + c, :], src, ACT.Copy,
                                    scale=0.125 if kind == "q" else 1.0)
                    ins.then_inc(q_evac, 1)

                for j, tile in enumerate(ph["tiles"]):
                    kind, g, *rest = tile
                    slot = (at["t"] + j) % RING
                    split(ph, 0, j)
                    products(ph, 0, j)
                    both = ps[:, 2 * slot:2 * slot + 2, 0:T]
                    if kind in "qk":
                        if normed:
                            if q > 0:
                                act.wait_ge(q_ss, q)
                            A(head_sq[:].rearrange("p (b f) -> p b f", b=2), both, ACT.Square).then_inc(q_sq, 1)
                            act.wait_ge(q_ss, q + 1)
                            A(head_std[:], head_sum[:], ACT.Sqrt, scale=1.0 / HD, bias=eps).then_inc(q_std, 1)
                        else:
                            if j >= RING:
                                act.wait_ge(q_turned, at["q"] + sum(k in "qk" for k, *_ in ph["tiles"][:j - 2]))
                            A(staging[:, slot, :].rearrange("p (b f) -> p b f", b=2), both,
                              ACT.Copy).then_inc(v_evac, 1)
                    elif kind == "f":
                        A(fT[:, 2 * g:2 * g + 2, :], both, ACT.Copy).then_inc(v_evac, 1)
                    elif which == "od":
                        A((v if who == "lat" else vc)[:, :, g * 256:g * 256 + 256], both, ACT.Copy).then_inc(v_evac, 1)
                    else:
                        jj = rest[0]
                        A(dv[:, g, :, jj * 256:jj * 256 + 256], both, ACT.Copy).then_inc(v_evac, 1)
                    if waiting is not None:
                        evac(*waiting)
                        waiting = None
                    if kind in "qk":
                        waiting = (q, tile)
                        q += 1
                if waiting is not None:
                    evac(*waiting)

            def fourier(ph):
                f = ph["at"]["fo"]
                for g in range(5):
                    if g < 4:
                        act.wait_ge(fo_ab, f + g + 1)
                        if g >= 2:
                            act.wait_ge(fo_mix, f + g - 1)
                        A(fab[:, g % 2].rearrange("p b f -> p (b f)"), ps[:, g % 2, :], ACT.Copy).then_inc(fo_cp, 1)
                    if g >= 1:
                        h = g - 1
                        act.wait_ge(fo_mix, f + h + 1)
                        A(H_hi[:, h, :], ps[:, 2 + h % 2, 0:T], ACT.Copy).then_inc(fo_hi, 1)

            def attend(ph):
                u0, n, which = ph["at"]["u"], ph["units"], ph["which"]
                prob = prob_d if which == "dil" else prob_a
                width = {"ev": 4 if ph["who"] == "lat" else 2, "od": 4, "dil": 6}[which] * P
                for u in range(n + 1):
                    if u < n:
                        s = small[:, (u0 + u) % 4]
                        act.wait_ge(s_max, u0 + u + 1)
                        if which == "ev":
                            A(prob[:, u % 2, 0:width], prob[:, u % 2, 0:width], ACT.Exp, bias=s[:, 2:3],
                              accum_out=s[:, 3:4])
                            A(s[:, 4:5], par("sink", u // 2), ACT.Exp, bias=s[:, 2:3]).then_inc(p_exp, 1)
                        else:
                            A(prob[:, u % 2, 0:width], prob[:, u % 2, 0:width], ACT.Exp, bias=s[:, 2:3],
                              accum_out=s[:, 3:4]).then_inc(p_exp, 1)
                    if u >= 1:
                        w = u - 1
                        act.wait_ge(pt_done, u0 + w + 1)
                        if w >= 2:
                            act.wait_ge(o_done, u0 + w - 1)
                        A(probT[:, w % 2, 0:width], ps[:, 4:6, :].rearrange("p b f -> p (b f)")[:, 0:width],
                          ACT.Copy).then_inc(pt_copy, 1)
                hi = S_hi if which == "dil" else H_hi
                first = {"ev": 4, "od": 0, "dil": 4 * ph.get("half", 0)}[which]
                for k in range(ph["banks"]):
                    act.wait_ge(ot_done, ph["at"]["ot"] + k + 1)
                    A(hi[:, first + 2 * k:first + 2 * k + 2, :], ps[:, k, :].rearrange("p (c t) -> p c t", c=2),
                      ACT.Copy).then_inc(ot_hi, 1)

            def gemm_b(ph):
                in_loop(act, ph["chunks"] // 2, lambda i, j: split(ph, i, j))

            def ffn_a(ph):
                def step(i, j):
                    slot = (ph["at"]["t"] + j) % RING
                    split(ph, i, j)
                    products(ph, i, j)
                    A(sil[:, slot, 0:T], ps[:, 2 * slot, 0:T], ACT.Silu).then_inc(f_sil, 1)
                in_loop(act, FC, step)

            def ret(ph):
                at, r = ph["at"], ph["at"]["rt"]
                for j in range(16):
                    slot = (at["t"] + j) % RING
                    split(ph, 0, j)
                    if j >= 8:
                        products(ph, 0, j)
                        A(rv[:, :, (j - 8) * 256:(j - 7) * 256], ps[:, 2 * slot:2 * slot + 2, 0:T],
                          ACT.Copy).then_inc(v_evac, 1)
                for h in range(RET_H):
                    act.wait_ge(r_arg, RET_H * r + h + 1)
                    A(rD[:, h], rD[:, h], ACT.Exp).then_inc(r_D, 1)
                for h in range(RET_H + 1):
                    if h < RET_H:
                        b0 = 4 + 2 * (h % 2)
                        act.wait_ge(r_o, RET_H * r + h + 1)
                        src = ps[:, b0:b0 + 2, :].rearrange("p b (e t) -> p (b e) t", e=2)
                        A(ro[:, 4 * h:4 * h + 4, :], src, ACT.Copy).then_inc(r_cp, 1)
                        if h >= 2:
                            act.wait_ge(r_sum, RET_H * r + h - 1)
                        A(rsq[:, h % 2], src, ACT.Square).then_inc(r_cp, 1)
                    if h >= 1:
                        g = h - 1
                        act.wait_ge(r_sum, RET_H * r + g + 1)
                        if g >= 1:
                            act.wait_ge(r_on, RET_H * r + g)
                        A(rstd[:], ps[:, 2 + g % 2, 0:T], ACT.Sqrt, scale=1.0 / RET_DV,
                          bias=eps).then_inc(r_std, 1)
                for j in range(16, 24):
                    slot = (at["t"] + j) % RING
                    split(ph, 0, j)
                    products(ph, 0, j)
                    if j >= 19:
                        act.wait_ge(r_gate, 8 * r + j - 18)
                    A(sil[:, slot, :].rearrange("p (c t) -> p c t", c=2), ps[:, 2 * slot:2 * slot + 2, 0:T],
                      ACT.Silu).then_inc(v_evac, 1)

            def conv(ph):
                for j in range(8):
                    slot = (ph["at"]["t"] + j) % RING
                    split(ph, 0, j)
                    products(ph, 0, j)
                    A(sil[:, slot, 0:T], ps[:, 2 * slot + 1, 0:T], ACT.Sigmoid,
                      bias=par("conv_b_in", C + j)).then_inc(c_sg, 1)
                for c in range(CONV_V, C):
                    for k in range(TAPS):
                        n = (c - CONV_V) * TAPS + k
                        if n >= DIAGS:
                            act.wait_ge(diag_used, n - DIAGS + 1)
                        A(taps_diag[:, n % DIAGS, :], ident, ACT.Copy,
                          scale=par("conv_w_dw", k * C + c)).then_inc(diag_made, 1)
                for c in range(CONV_V, C):
                    act.wait_ge(diag_used, (c - CONV_V + 1) * TAPS)
                    A(cv[:, c, :], ps[:, c - CONV_V, 0:T], ACT.Identity,
                      bias=par("conv_b_dw", c)).then_inc(c_tensor, 1)
                for c in range(C):
                    act.wait_ge(c_dev, c + 1)
                    A(sq[:, c, :], cv[:, c, :], ACT.Square).then_inc(c_sq, 1)
                act.wait_ge(c_var, 1)
                A(rstd[:], ps[:, 7, 0:T], ACT.Sqrt, scale=1.0 / D, bias=ln_eps).then_inc(c_std, 1)
                for c in range(C):
                    act.wait_ge(c_t, c + 1)
                    A(cv[:, c, :], cv[:, c, :], ACT.Silu, scale=par("conv_ln_g", c),
                      bias=par("conv_ln_b", c)).then_inc(c_y, 1)
                for c in range(C):
                    act.wait_ge(c_y, c + 1)
                    A(H_hi[:, c, :], cv[:, c, :], ACT.Copy).then_inc(c_y, 1)

            for ph in plan:
                {"setup": setup, "ada": ada, "norm": norm, "qkv": qkv, "fourier": fourier,
                 "attend": attend, "gemm_b": gemm_b, "ffn_a": ffn_a, "ret": ret, "conv": conv}.get(
                     ph["kind"], lambda _: None)(ph)

        @block.vector
        def _(dve):
            V = nc.vector
            dve_n = [0]

            def link(ins):
                dve_n[0] += 1
                ins.then_inc(dve_c, 1)
                dve.wait_ge(dve_c, dve_n[0])

            def split(ph, i, j):
                t0 = ph["at"]["t"] + AHEAD
                tile = t0 + RING * i + j
                if isinstance(tile, int) and tile >= NT:
                    return
                slot = (t0 + j) % RING
                dve.wait_ge(hi_done, tile + 1)
                V.tensor_tensor(w_lo[:, slot, :], w_raw[:, slot, :], whole(w_hi)[:, slot, :],
                                ALU.subtract).then_inc(lo_done, 1)

            def products(ph, i, j):
                dve.wait_ge(tile_done, ph["at"]["t"] + RING * i + j + 2)

            def setup(ph):
                V.memset(whole(c_wide)[:], 0.0).then_inc(c_zeroed, 1)
                dve.sem_inc(a_evac, RING)
                dve.sem_inc(ada_evac, RING)
                dve.wait_ge(c_rounded, 1)
                V.tensor_tensor(c_wide[:, :, 2:4], c_silu[:], whole(c_wide)[:, :, 0:2],
                                ALU.subtract).then_inc(setup_done, 1)
                for tile in range(AHEAD):
                    dve.wait_ge(hi_done, tile + 1)
                    V.tensor_tensor(w_lo[:, tile, :], w_raw[:, tile, :], whole(w_hi)[:, tile, :],
                                    ALU.subtract).then_inc(lo_done, 1)

            def ada(ph):
                l = ph["l"]
                raw = mod[:, l].rearrange("p (t c) w -> p t (c w)", c=2)

                def step(i, j):
                    slot = (ph["at"]["t"] + j) % RING
                    split(ph, i, j)
                    products(ph, i, j)
                    o = RING * i + j
                    dst = raw[:, o, :] if isinstance(o, int) else raw[:, bass.ds(o, 1), :].rearrange("p a x -> p (a x)")
                    V.tensor_copy(dst, ps[:, 3 + slot, 0:4]).then_inc(ada_evac, 1)
                in_loop(dve, 24, step)
                dve.wait_ge(ada_evac, RING + 24 * (l + 1))
                b = par("ada_b", 48 * l, 48).rearrange("p (c o) -> p c o", o=1).broadcast_to([P, 48, 2])
                link(V.tensor_tensor(mod[:, l], mod[:, l], b, ALU.add))
                for which in range(2):
                    g = par("norm1_g" if which == 0 else "norm2_g", C * l, C)
                    g = g.rearrange("p (c o) -> p c o", o=1).broadcast_to([P, C, 2])
                    scale = mod[:, l, 24 * which + C:24 * which + 2 * C, :]
                    link(V.tensor_scalar(mod_g[:, l, which], scale, 1.0, None, ALU.add))
                    ins = V.tensor_tensor(mod_g[:, l, which], mod_g[:, l, which], g, ALU.mult)
                ins.then_inc(ada_done, 1)
                dve.wait_ge(ada_done, l + 1)

            def norm(ph):
                n, src = ph["at"]["n"], res[ph["src"]]
                dve.wait_ge(n_std, n + 1)
                link(V.reciprocal(tok_inv[:], tok_std[:]))
                V.tensor_tensor(diag[:], ident.rearrange("p (o t) -> p o t", o=1).broadcast_to([P, 2, P]),
                                tok_inv[:].rearrange("p (b o) -> p b o", o=1).broadcast_to([P, 2, P]),
                                ALU.mult).then_inc(n_diag, 1)
                dve.wait_ge(n_bcast, n + 1)
                factor = ps[:, 1:2, 0:T].broadcast_to([P, 2, T])
                if ph["how"] == "post":
                    for c in range(4):
                        V.tensor_tensor(M[:, 2 * c:2 * c + 2, :], M[:, 2 * c:2 * c + 2, :], factor,
                                        ALU.mult).then_inc(n_t, 1)
                    for c in range(C):
                        dve.wait_ge(n_t, 4 * n + c // 2 + 1)
                        V.scalar_tensor_tensor(out=X[:, c, :], in0=M[:, c, :], scalar=par("norm_w", ph["w"] * C + c),
                                               in1=X[:, c, :], op0=ALU.mult, op1=ALU.add).then_inc(x_up, 1)
                    return
                for c in range(4):
                    V.tensor_tensor(sq[:, 2 * c:2 * c + 2, :], src[:, 2 * c:2 * c + 2, :], factor,
                                    ALU.mult).then_inc(n_t, 1)
                m = C * sum(p["kind"] == "norm" and p["how"] != "post" for p in plan[:plan.index(ph)])
                for c in range(C):
                    dve.wait_ge(n_hi, m + c + 1)
                    if ph["how"] == "ada":
                        w, l, which = col[ph["src"]], ph["l"], ph["which"]
                        link(V.tensor_scalar(sq[:, c, :], sq[:, c, :], mod_g[:, l, which, c, w:w + 1],
                                             mod[:, l, 24 * which + c, w:w + 1], ALU.mult, ALU.add))
                        V.tensor_tensor(H_lo[:, c, :], sq[:, c, :], whole(H_hi)[:, c, :],
                                        ALU.subtract).then_inc(n_lo, 1)
                    else:
                        V.scalar_tensor_tensor(out=H_lo[:, c, :], in0=sq[:, c, :],
                                               scalar=par("norm_w", ph["w"] * C + c),
                                               in1=whole(H_hi)[:, c, :], op0=ALU.mult,
                                               op1=ALU.subtract).then_inc(n_lo, 1)

            def qkv(ph):
                at, which, who = ph["at"], ph["which"], ph["who"]
                q = at["q"]
                for j, tile in enumerate(ph["tiles"]):
                    kind, g, *rest = tile
                    slot = (at["t"] + j) % RING
                    split(ph, 0, j)
                    if kind not in "qk":
                        continue
                    if which == "dil":
                        dil_rope(ph, j, slot)
                        q += 1
                        continue
                    dve.wait_ge(q_sq, q + 1)
                    V.tensor_reduce(head_sum[:], head_sq[:].rearrange("p (h d) -> p h d", d=HD), AX.X,
                                    ALU.add).then_inc(q_ss, 1)
                    dve.wait_ge(q_std, q + 1)
                    link(V.reciprocal(head_inv[:], head_std[:]))
                    turned = at["q"] + sum(x[0] in "qk" for x in ph["tiles"][:max(0, j - 2)])
                    if turned:
                        dve.wait_ge(q_turned, turned)
                    st = stage[:, slot, :].rearrange("p (h d) -> p h d", d=HD)
                    inv = head_inv[:].rearrange("p (h o) -> p h o", o=1).broadcast_to([P, 8, HD])
                    for b in range(2):
                        ins = V.tensor_tensor(st[:, 4 * b:4 * b + 4], ps[:, 2 * slot + b, 0:T].rearrange(
                            "p (h d) -> p h d", d=HD), inv[:, 4 * b:4 * b + 4], ALU.mult)
                        if b == 0 or which == "ev":
                            link(ins)
                    if which == "od":
                        ins.then_inc(q_staged, 1)
                    else:
                        ev_finish(ph, kind, slot, who)
                    q += 1

            def ev_finish(ph, kind, slot, who):
                st4 = stage[:, slot, :].rearrange("p (b h d) -> p b h d", b=2, d=HD)
                nh = 4 if kind == "q" else 2
                gain = par("ev_q_g" if kind == "q" else "ev_k_g", 0, HD)
                gain = gain.rearrange("p (o d) -> p o d", o=1).broadcast_to([P, nh, HD])
                if kind == "k":
                    vv = ev_v if who == "lat" else ev_vc
                    link(V.tensor_copy(vv[:], ps[:, 2 * slot:2 * slot + 2, P:2 * P]))
                for b in range(2):
                    ins = V.tensor_tensor(st4[:, b, 0:nh], st4[:, b, 0:nh], gain, ALU.mult)
                    if b == 0 or who == "lat" or kind == "k":
                        link(ins)
                if who == "lat":
                    for b in range(2):
                        cos = con("ev_cos").rearrange("p (b d) -> p b d", b=2)[:, b:b + 1, :].broadcast_to([P, nh, HD])
                        sin = con("ev_sin").rearrange("p (b r x d) -> p b r x d", b=2, r=2, x=2)[:, b]
                        x = st4[:, b, 0:nh].rearrange("p h (r x d) -> p h r x d", r=2, x=2)
                        ra = rope_t[:, 0, 0:nh * HD].rearrange("p (h d) -> p h d", d=HD)
                        rb = rope_t[:, 1, 0:nh * HD].rearrange("p (h r x d) -> p h r x d", r=2, x=2, d=16)
                        link(V.tensor_tensor(ra, st4[:, b, 0:nh], cos, ALU.mult))
                        for y in range(2):
                            for r in range(2):
                                sn = sin[:, r:r + 1, y, :].broadcast_to([P, nh, 16])
                                link(V.tensor_tensor(rb[:, :, r, y, :], x[:, :, r, 1 - y, :], sn, ALU.mult))
                        ins = V.tensor_tensor(st4[:, b, 0:nh], ra,
                                              rope_t[:, 1, 0:nh * HD].rearrange("p (h d) -> p h d", d=HD), ALU.add)
                        if b == 0 or kind == "k":
                            link(ins)
                if kind == "k":
                    for b in range(2):
                        link(V.tensor_copy(st4[:, b, 3], st4[:, b, 1]))
                        link(V.tensor_copy(st4[:, b, 2], st4[:, b, 1]))
                        ins = V.tensor_copy(st4[:, b, 1], st4[:, b, 0])
                        if b == 0:
                            link(ins)
                ins.then_inc(q_staged, 1)

            def dil_rope(ph, j, slot):
                at = ph["at"]
                dve.wait_ge(v_evac, at["ea"] + j + 1 + RING)
                st = dstage[:, slot, :].rearrange("p (b h d) -> p b h d", b=2, d=HD)
                cos = con("dil_cos").rearrange("p (b o d) -> p b o d", b=2, o=1)
                sin = con("dil_sin").rearrange("p (b o d) -> p b o d", b=2, o=1)
                ra = dil_t[:, 0].rearrange("p (b h d) -> p b h d", b=2, d=16)
                rb = dil_t[:, 1].rearrange("p (b h d) -> p b h d", b=2, d=16)
                V.tensor_tensor(ra, st[:, :, :, 0:16], cos.broadcast_to([P, 2, 4, 16]), ALU.mult)
                V.tensor_tensor(rb[:, :, :, 0:8], st[:, :, :, 8:16], sin[:, :, :, 0:8].broadcast_to([P, 2, 4, 8]),
                                ALU.mult)
                link(V.tensor_tensor(rb[:, :, :, 8:16], st[:, :, :, 0:8],
                                     sin[:, :, :, 8:16].broadcast_to([P, 2, 4, 8]), ALU.mult))
                V.tensor_tensor(st[:, :, :, 0:16], ra, rb, ALU.add).then_inc(q_staged, 1)
                q = at["q"] + sum(k in "qk" for k, *_ in ph["tiles"][:j])
                dve.wait_ge(q_staged, q + 1)

            def fourier(ph):
                for g in range(4):
                    dve.wait_ge(fo_hi, ph["at"]["fo"] + g + 1)
                    V.tensor_tensor(H_lo[:, g, :], ps[:, 2 + g % 2, 0:T], whole(H_hi)[:, g, :],
                                    ALU.subtract).then_inc(fo_lo, 1)

            def attend(ph):
                u0, n, which = ph["at"]["u"], ph["units"], ph["which"]
                prob = prob_d if which == "dil" else prob_a
                lat = ph["who"] == "lat"
                outs = dO if which == "dil" else O
                zeros = win_mask[:, 0, T:2 * T]

                def add_max(u, cols, src, mask, at):
                    return V.tensor_tensor_reduce(out=prob[:, u % 2, cols], in0=src, in1=mask, scale=1.0,
                                                  scalar=-3.0e38, op0=ALU.add, op1=ALU.max, accum_out=at)

                for u in range(n + 2):
                    if u < n:
                        h, b = u // 2, u % 2
                        s = small[:, (u0 + u) % 4]
                        bank = 2 * (u % 2)
                        dve.wait_ge(s_done, u0 + u + 1)
                        if u >= 2:
                            dve.wait_ge(pt_done, u0 + u - 1)
                        if which == "ev":
                            w = 2 * T if lat else T
                            mask = win_mask[:, b, :] if lat else zeros
                            link(add_max(u, slice(0, w), ps[:, bank, 0:w], mask, s[:, 0:1]))
                            V.tensor_scalar(s[:, 2:3], s[:, 0:1], par("sink", h), -1.0, ALU.max,
                                            ALU.mult).then_inc(s_max, 1)
                        elif which == "od":
                            dve.wait_ge(b_masked, h + 1)
                            tbl = bias[:, h % 4, (2 - 2 * b) * GW:(6 - 2 * b) * GW]
                            add_max(u, slice(0, T), ps[:, bank, 0:T], tbl, s[:, 0:1])
                            link(add_max(u, slice(T, 2 * T), ps[:, bank, T:2 * T], zeros, s[:, 1:2]))
                            V.tensor_scalar(s[:, 2:3], s[:, 0:1], s[:, 1:2], -1.0, ALU.max,
                                            ALU.mult).then_inc(s_max, 1)
                        else:
                            flat = ps[:, bank:bank + 2, :].rearrange("p b f -> p (b f)")[:, 0:3 * T]
                            link(add_max(u, slice(0, 3 * T), flat, dil_mask[:, b, :], s[:, 0:1]))
                            V.tensor_scalar(s[:, 2:3], s[:, 0:1], -1.0, None, ALU.mult).then_inc(s_max, 1)
                    if u >= 2:
                        w = u - 2
                        h, b = w // 2, w % 2
                        s = small[:, (u0 + w) % 4]
                        dve.wait_ge(o_done, u0 + w + 1)
                        if which == "ev":
                            link(V.tensor_tensor(s[:, 3:4], s[:, 3:4], s[:, 4:5], ALU.add))
                        link(V.reciprocal(s[:, 5:6], s[:, 3:4]))
                        V.tensor_scalar(outs[:, b, 64 * h:64 * h + 64], ps[:, 6 + w % 2, 0:64], s[:, 5:6],
                                        None, ALU.mult).then_inc(o_evac, 1)
                hi, lo = (S_hi, S_lo) if which == "dil" else (H_hi, H_lo)
                first = {"ev": 4, "od": 0, "dil": 4 * ph.get("half", 0)}[which]
                for k in range(ph["banks"]):
                    dve.wait_ge(ot_hi, ph["at"]["ot"] + k + 1)
                    V.tensor_tensor(lo[:, first + 2 * k:first + 2 * k + 2, :],
                                    ps[:, k, :].rearrange("p (c t) -> p c t", c=2),
                                    whole(hi)[:, first + 2 * k:first + 2 * k + 2, :],
                                    ALU.subtract).then_inc(ot_lo, 1)

            def gemm_b(ph):
                at = ph["at"]
                n = ph["chunks"] // 2
                in_loop(dve, n, lambda i, j: split(ph, i, j))
                for c in range(C):
                    if c < C - 1:
                        dve.wait_ge(b_done, (C - 1) * at["b"] + c + 1)
                    else:
                        dve.wait_ge(tile_done, at["t"] + n + 1)
                    if ph["evac"] == "gate":
                        r, w = res[ph["who"]], col[ph["who"]]
                        V.scalar_tensor_tensor(out=r[:, c, :], in0=ps[:, c, 0:T],
                                               scalar=mod[:, ph["l"], C * ph["g"] + c, w:w + 1],
                                               in1=r[:, c, :], op0=ALU.mult, op1=ALU.add).then_inc(x_up, 1)
                    elif ph["evac"] == "mb":
                        V.tensor_scalar(M[:, c, :], ps[:, c, 0:T], par("conv_b_out", c), None,
                                        ALU.add).then_inc(m_evac, 1)
                    else:
                        V.tensor_copy(M[:, c, :], ps[:, c, 0:T]).then_inc(m_evac, 1)

            def ffn_a(ph):
                f = ph["at"]["f"]

                def step(i, j):
                    slot = (ph["at"]["t"] + j) % RING
                    split(ph, i, j)
                    dve.wait_ge(f_sil, f + RING * i + j + 1)
                    dve.wait_ge(f_split, f + RING * i + j + 1)
                    V.tensor_tensor(a32[:, slot, :], sil[:, slot, 0:T], ps[:, 2 * slot + 1, 0:T],
                                    ALU.mult).then_inc(a_evac, 1)
                in_loop(dve, FC, step)

            def ret(ph):
                at, r = ph["at"], ph["at"]["rt"]
                for j in range(16):
                    slot = (at["t"] + j) % RING
                    split(ph, 0, j)
                    if j >= 8:
                        continue
                    products(ph, 0, j)
                    dst = (rq if j < 4 else rk)[:, 2 * (j % 4):2 * (j % 4) + 2, :]
                    both = ps[:, 2 * slot:2 * slot + 2, 0:T]
                    cos = con("ret_cos").rearrange("p (o t) -> p o t", o=1).broadcast_to([P, 2, T])
                    pc = rtmp[:, 0, :].rearrange("p (c t) -> p c t", c=2)
                    V.tensor_tensor(pc, both, cos, ALU.mult)
                    V.tensor_tensor(rtmp[:, 1, 0:T], both[:, 1, :], con("ret_sin"), ALU.mult)
                    V.tensor_tensor(rtmp[:, 1, T:2 * T], both[:, 0, :], con("ret_sin"), ALU.mult).then_inc(a_evac, 1)
                    dve.wait_ge(a_evac, at["ed"] + j + 1 + RING)
                    V.tensor_tensor(dst[:, 0, :], rtmp[:, 0, 0:T], rtmp[:, 1, 0:T], ALU.subtract)
                    V.tensor_tensor(dst[:, 1, :], rtmp[:, 0, T:2 * T], rtmp[:, 1, T:2 * T],
                                    ALU.add).then_inc(r_rope, 1)
                    dve.wait_ge(r_rope, 8 * r + j + 1)
                for h in range(RET_H + 2):
                    if h < RET_H:
                        dve.wait_ge(r_s, RET_H * r + h + 1)
                        dve.wait_ge(r_D, RET_H * r + h + 1)
                        if h >= 1:
                            dve.wait_ge(r_o, RET_H * r + h)
                        V.scalar_tensor_tensor(out=rst[:], in0=ps[:, 0:2, 0:T], scalar=RET_DK ** -0.5,
                                               in1=rD[:, h], op0=ALU.mult, op1=ALU.mult).then_inc(r_st, 1)
                    if h >= 2:
                        g = h - 2
                        dve.wait_ge(r_std, RET_H * r + g + 1)
                        link(V.reciprocal(rstd[:], rstd[:]))
                        V.tensor_tensor(ro[:, 4 * g:4 * g + 4, :], ro[:, 4 * g:4 * g + 4, :],
                                        rstd[:].rearrange("p (o t) -> p o t", o=1).broadcast_to([P, 4, T]),
                                        ALU.mult).then_inc(r_on, 1)
                for j in range(16, 24):
                    slot = (at["t"] + j) % RING
                    split(ph, 0, j)
                    dve.wait_ge(v_evac, at["ea"] + j - 8 + 1 + RING)
                    dve.wait_ge(r_on, RET_H * (r + 1))
                    o = ro[:, 2 * (j - 16):2 * (j - 16) + 2, :]
                    V.tensor_tensor(o, sil[:, slot, :].rearrange("p (c t) -> p c t", c=2), o,
                                    ALU.mult).then_inc(r_gate, 1)

            def conv(ph):
                at = ph["at"]
                V.memset(upad[:, :, 0:PAD], 0.0)
                V.memset(upad[:, :, PAD + T:], 0.0).then_inc(padded, 1)
                def tap(c, k):
                    src, w = upad[:, c, k:k + T], par("conv_w_dw", k * C + c)
                    done = c_conv if k == TAPS - 1 else taps
                    if k == 0:
                        V.tensor_scalar(cv[:, c, :], src, w, par("conv_b_dw", c), ALU.mult,
                                        ALU.add).then_inc(done, 1)
                    else:
                        dve.wait_ge(taps, (TAPS - 1) * c + k)
                        V.scalar_tensor_tensor(out=cv[:, c, :], in0=src, scalar=w, in1=cv[:, c, :],
                                               op0=ALU.mult, op1=ALU.add).then_inc(done, 1)

                todo = [(c, k) for c in range(CONV_V) for k in range(TAPS)]
                for j in range(8):
                    slot = (at["t"] + j) % RING
                    split(ph, 0, j)
                    dve.wait_ge(c_sg, j + 1)
                    V.scalar_tensor_tensor(out=upad[:, j, PAD:PAD + T], in0=ps[:, 2 * slot, 0:T],
                                           scalar=par("conv_b_in", j), in1=sil[:, slot, 0:T], op0=ALU.add,
                                           op1=ALU.mult).then_inc(a_evac, 1)
                    if j == 0:
                        dve.wait_ge(padded, 1)
                    dve.wait_ge(a_evac, RING + at["ed"] + j + 1)
                    for _ in range(6):
                        tap(*todo.pop(0))
                for c, k in todo:
                    tap(c, k)
                dve.wait_ge(c_tensor, C - CONV_V)
                dve.wait_ge(c_mean, 1)
                mean = rstd
                link(V.tensor_scalar(mean[:], ps[:, 6, 0:T], 1.0 / D, None, ALU.mult))
                for c in range(C):
                    V.tensor_tensor(cv[:, c, :], cv[:, c, :], mean[:], ALU.subtract).then_inc(c_dev, 1)
                dve.wait_ge(c_std, 1)
                link(V.reciprocal(rstd[:], rstd[:]))
                for c in range(C):
                    V.tensor_tensor(cv[:, c, :], cv[:, c, :], rstd[:], ALU.mult).then_inc(c_t, 1)
                for c in range(C):
                    dve.wait_ge(c_y, C + c + 1)
                    V.tensor_tensor(H_lo[:, c, :], cv[:, c, :], whole(H_hi)[:, c, :],
                                    ALU.subtract).then_inc(c_lo, 1)

            for ph in plan:
                {"setup": setup, "ada": ada, "norm": norm, "qkv": qkv, "fourier": fourier,
                 "attend": attend, "gemm_b": gemm_b, "ffn_a": ffn_a, "ret": ret, "conv": conv}.get(
                     ph["kind"], lambda _: None)(ph)

        @block.gpsimd
        def _(pool):
            G = nc.gpsimd
            pool_n = [0]

            def link(ins):
                pool_n[0] += 1
                ins.then_inc(pool_c, 1)
                pool.wait_ge(pool_c, pool_n[0])

            def ffn_a(ph):
                at = ph["at"]

                def step(i, j):
                    slot = (at["t"] + j) % RING
                    o = RING * i + j
                    if isinstance(o, int):
                        hi, lo, hi32 = A_hi[:, o, :], A_lo[:, o, :], whole(A_hi)[:, o, :]
                    else:
                        one = lambda x: x[:, bass.ds(o, 1), :].rearrange("p a t -> p (a t)")
                        hi, lo, hi32 = one(A_hi), one(A_lo), one(whole(A_hi))
                    pool.wait_ge(a_evac, at["ed"] + o + 1 + RING)
                    G.tensor_copy(hi, a32[:, slot, :]).then_inc(f_hi, 1)
                    pool.wait_ge(f_hi, at["f"] + o + 1)
                    G.tensor_tensor(lo, a32[:, slot, :], hi32, ALU.subtract).then_inc(f_split, 1)
                in_loop(pool, FC, step)

            def ret(ph):
                r = ph["at"]["rt"]
                pool.wait_ge(r_lg, 1)
                pool.wait_ge(n_lo, C * sum(p["kind"] == "norm" and p["how"] != "post"
                                           for p in plan[:plan.index(ph)]))
                for h in range(RET_H):
                    f, b = (2 * r) * RET_H + h, (2 * r + 1) * RET_H + h
                    pos = con("dpos").rearrange("p (b t) -> p b t", b=2)
                    neg = con("dneg").rearrange("p (b t) -> p b t", b=2)
                    link(G.tensor_scalar(rD[:, h], pos, decay[:, f:f + 1], None, ALU.mult))
                    link(G.tensor_scalar(rarg[:], neg, decay[:, b:b + 1], None, ALU.mult))
                    G.tensor_tensor(rD[:, h], rD[:, h], rarg[:], ALU.add).then_inc(r_arg, 1)
                    pool.wait_ge(r_arg, RET_H * r + h + 1)
                for j in range(8):
                    pool.wait_ge(r_gate, 8 * r + j + 1)
                    o = slice(2 * j, 2 * j + 2)
                    link(G.tensor_scalar(A_hi[:, o, :], ro[:, o, :], 1.0, None, ALU.mult))
                    G.tensor_tensor(A_lo[:, o, :], ro[:, o, :], whole(A_hi)[:, o, :],
                                    ALU.subtract).then_inc(r_split, 1)

            def attend(ph):
                if ph["which"] != "od":
                    return
                step = 2 * NA_KW - 1
                pool.wait_ge(q_evac, ph["at"]["q"])
                for h in range(NA_H + 1):
                    if h < NA_H:
                        if h >= 2:
                            pool.wait_ge(b_masked, h - 1)
                        for half in range(2):
                            first = (h * (2 * NA_KH - 1) + 5 - half) * step + NA_KW - GW
                            src = bass.AP(rel_bias.tensor, first, [[1, GW], [step, 6], [1, GW]])
                            G.dma_start(bias_raw[h % 2][half * GW:half * GW + GW].rearrange(
                                "p (d k) -> p d k", k=GW), src).then_inc(b_loaded[h % 2], 16)
                    if h >= 1:
                        g = h - 1
                        pool.wait_ge(b_loaded[g % 2], 32 * (g // 2 + 1))
                        if g >= 4:
                            pool.wait_ge(s_max, ph["at"]["u"] + 2 * (g - 4) + 2)
                        m = con("na_mask").rearrange("p (o k) -> p o k", o=1).broadcast_to([P, 6, GW])
                        raw = bias_raw[g % 2][:].rearrange("p (d k) -> p d k", k=GW)
                        G.tensor_tensor(bias[:, g % 4].rearrange("p (d k) -> p d k", k=GW),
                                        raw[:, :, ::-1], m, ALU.add).then_inc(b_masked, 1)

            pool.sem_inc(f_split, RING)
            for ph in plan:
                {"attend": attend, "ffn_a": ffn_a, "ret": ret}.get(ph["kind"], lambda _: None)(ph)


def tiles_a(w):
    n = w.shape[1] // 256
    return w.reshape(C, P, n, 256).transpose(2, 1, 0, 3).reshape(n, P, TW)


def tiles_b(w):
    n = w.shape[0] // 256
    return w.reshape(n, 2, P, D).transpose(0, 2, 1, 3).reshape(n, P, TW)


def tiles_pair(w1, w2):
    both = np.stack([w1.reshape(D, -1, P), w2.reshape(D, -1, P)], 2)
    return tiles_a(both.reshape(D, -1))


def chunked(a):
    return a.reshape(-1, P).T


def lay_out(i):
    i = {k: np.asarray(a) for k, a in i.items()}
    w = []
    for l in range(2):
        w.append(tiles_a(i["ada_w"][l]))
    w.append(tiles_a(i["ev_w_in"][0]))
    w.append(tiles_b(i["ev_w_out"][0]))

    def ffn1(l):
        return [tiles_pair(i["ffn_w_gate"][l], i["ffn_w_up"][l]), tiles_b(i["ffn_w_down"][l])]

    def ffn2(l):
        a = i["ffn_w_in_2"][l]
        return [tiles_pair(a[:, :FF], a[:, FF:]), tiles_b(i["ffn_w_out_2"][l])]

    w += ffn1(0)
    w.append(tiles_a(i["od_w_in"][0]))
    w.append(tiles_b(i["od_w_out"][0]))
    w += ffn1(1)
    w += [tiles_a(i["ret_w_in_2"][0]), tiles_b(i["ret_w_out_2"][0])] + ffn2(0)
    cw = i["conv_w_in_2"][0]
    w += [tiles_pair(cw[:, :D], cw[:, D:]), tiles_b(i["conv_w_out_2"][0])] + ffn2(1)
    att = i["attn_w_in_2"][0].reshape(D, 3, 3, 2, 512)
    w += [tiles_a(att[:, :, :, half].reshape(D, -1)) for half in range(2)]
    w += [tiles_b(i["attn_w_out_2"][0])] + ffn2(2)
    w += [tiles_a(i["ret_w_in_2"][1]), tiles_b(i["ret_w_out_2"][1])] + ffn2(3)
    weights = np.ascontiguousarray(np.concatenate(w))
    assert weights.shape == (TILES, P, TW)
    rep = lambda a: np.broadcast_to(a.reshape(1, -1), (P, a.size))
    cc = np.stack([i["c"][0], i["c_ctx"]], 1)
    p = {"c": cc.reshape(C, P, 2).transpose(1, 0, 2).reshape(P, -1), "ada_b": chunked(i["ada_b"]),
         "norm1_g": chunked(i["norm1_g"]), "norm2_g": chunked(i["norm2_g"]),
         "norm_w": chunked(i["norm_w_2"]), "conv_b_in": chunked(i["conv_b_in_2"]),
         "conv_b_dw": chunked(i["conv_b_dw_2"]), "conv_ln_g": chunked(i["conv_ln_g_2"]),
         "conv_ln_b": chunked(i["conv_ln_b_2"]), "conv_b_out": chunked(i["conv_b_out_2"]),
         "conv_w_dw": chunked(i["conv_w_dw_2"]),
         "od_q_g": np.concatenate([i["od_q_norm"][0]] * 2)[:, None],
         "od_k_g": np.concatenate([i["od_k_norm"][0]] * 2)[:, None],
         "ev_q_g": rep(i["ev_q_norm"]), "ev_k_g": rep(i["ev_k_norm"]), "sink": rep(i["ev_sink"]),
         "decay": rep(i["ret_log1m_decay_2"])}
    params = np.ascontiguousarray(np.concatenate([p[n] for n, _ in PARAMS], 1))
    assert params.shape == (P, PARAM_W)
    feature = lambda a: np.ascontiguousarray(a[0].T.reshape(C, P, T).transpose(1, 0, 2))
    return {"weights": weights, "x_in": feature(i["x"]), "ctx_in": feature(i["ctx"]),
            "params_in": params, "consts_in": constants(),
            "rel_bias": np.ascontiguousarray(i["od_rel_bias"][..., ::-1])}


def kernel(**inputs):
    import concourse.bacc as _bacc
    from concourse.bass_utils import run_bass_kernel_spmd as _run

    nc = _bacc.Bacc("TRN2", target_bir_lowering=False, num_devices=1)
    arrays, args = {}, {}
    for name, a in lay_out(inputs).items():
        arrays[f"{name}_dram"] = a
        args[name] = nc.dram_tensor(f"{name}_dram", a.shape, mybir.dt.from_np(a.dtype), kind="ExternalInput").ap()
    out = nc.dram_tensor("out_dram", (P, C, T), F32, kind="ExternalOutput").ap()
    two_blocks_kernel(nc, out=out, **args)
    r = _run(nc, [arrays], core_ids=[0])
    got = r.results[0]["out_dram"]
    return np.ascontiguousarray(got.transpose(1, 0, 2).reshape(D, T).T)[None]
```
